# Optimizing a Trainium2 kernel written in Bass

```python
import math
import jax, jax.numpy as jnp
from jax import lax
import numpy as np

D_MODEL = 1024
BATCH = 1
SEQ = 256
DEPTH = 2

GRID_W = 64
CTX_LEN = 256
Q_BLOCK = 128
EPS = 1e-6
ROPE_BASE = 10000.0
N_MOD = 6

SC_WIDTH = D_MODEL // 2
SC_IN = 3 * SC_WIDTH
SC_KERNEL = 3
MLA_V = 128
MLA_NOPE = 128
MLA_ROPE = 64
MLA_HEADS = (D_MODEL - SC_WIDTH) // MLA_V
MLA_Q_RANK = 3 * D_MODEL // 8
MLA_KV_RANK = D_MODEL // 4
EVEN_IN = SC_IN + MLA_Q_RANK + MLA_KV_RANK + MLA_ROPE
MLA_SCALE = (MLA_NOPE + MLA_ROPE) ** -0.5
DIFF_WIDTH = 3 * D_MODEL // 4
DIFF_HEAD = 64
DIFF_HEADS = DIFF_WIDTH // (2 * DIFF_HEAD)
DIFF_SCALE = DIFF_HEAD ** -0.5
FNET_WIDTH = D_MODEL - DIFF_WIDTH
FNET_GROUPS = 4
FNET_GROUP_DIM = FNET_WIDTH // FNET_GROUPS
ODD_IN = 3 * DIFF_WIDTH + FNET_WIDTH
D_FF = ((8 * D_MODEL // 3 + 127) // 128) * 128
N_EXPERTS = 8
TOP_K = 2

kernel_name = 'hybrid_diffusion_conv_mla_diffattn_fnet_moe'

def _rms_norm(x, g):
    xf = x.astype(jnp.float32)
    y = xf * lax.rsqrt(jnp.mean(xf * xf, axis=-1, keepdims=True) + EPS)
    return (y * g.astype(jnp.float32)).astype(x.dtype)

def _ada(cond, w, b):
    m = (jax.nn.silu(cond) @ w + b)[:, None, :]
    return jnp.split(m, N_MOD, axis=-1)

def _modulate(h, shift, scale):
    return h * (1 + scale) + shift

def _axial_rope(rows, rot_dim):
    row = jnp.repeat(jnp.arange(rows, dtype=jnp.float32), GRID_W)
    col = jnp.tile(jnp.arange(GRID_W, dtype=jnp.float32), rows)
    n_freq = rot_dim // 4
    inv = ROPE_BASE ** (-jnp.arange(n_freq, dtype=jnp.float32) / n_freq)
    ang = jnp.concatenate([row[:, None] * inv, col[:, None] * inv], axis=-1)
    return jnp.cos(ang), jnp.sin(ang)

def _apply_rope(x, rope):
    cos, sin = rope
    shape = (1, x.shape[1]) + (1,) * (x.ndim - 3) + (cos.shape[-1],)
    cos, sin = cos.reshape(shape), sin.reshape(shape)
    x1, x2 = jnp.split(x.astype(jnp.float32), 2, axis=-1)
    return jnp.concatenate([x1 * cos - x2 * sin, x1 * sin + x2 * cos], axis=-1).astype(x.dtype)

def _map_query_blocks(fn, q):
    B, T = q.shape[:2]
    nb = T // Q_BLOCK
    qb = jnp.moveaxis(q.reshape((B, nb, Q_BLOCK) + q.shape[2:]), 1, 0)
    out = lax.map(fn, qb)
    return jnp.moveaxis(out, 0, 1).reshape((B, T) + out.shape[3:])

def _swiglu(h, wg, wu, wd):
    return (jax.nn.silu(h @ wg) * (h @ wu)) @ wd

def _moe(h, router_w, w_gate, w_up, w_down):
    logits = (h @ router_w).astype(jnp.float32)
    top_v, top_i = lax.top_k(logits, TOP_K)
    top_w = jax.nn.softmax(top_v, axis=-1)
    gates = jnp.einsum('btk,btke->bte', top_w, jax.nn.one_hot(top_i, N_EXPERTS, dtype=jnp.float32)).astype(h.dtype)
    out = jnp.zeros_like(h)
    for e in range(N_EXPERTS):
        out = out + gates[..., e:e + 1] * _swiglu(h, w_gate[e], w_up[e], w_down[e])
    return out

def _short_conv(z, conv_w):
    b_gate, c_gate, u = jnp.split(z, 3, axis=-1)
    u = c_gate * u
    conv = lax.conv_general_dilated(u, conv_w[:, None, :], window_strides=(1,), padding=((SC_KERNEL // 2, SC_KERNEL // 2),),
                                    dimension_numbers=('NWC', 'WIO', 'NWC'), feature_group_count=SC_WIDTH)
    return b_gate * conv

def _mla_q(zq, q_norm_g, w_uq, rope):
    B, T = zq.shape[:2]
    q = (_rms_norm(zq, q_norm_g) @ w_uq).reshape(B, T, MLA_HEADS, MLA_NOPE + MLA_ROPE)
    q_nope, q_pe = q[..., :MLA_NOPE], q[..., MLA_NOPE:]
    if rope is not None:
        q_pe = _apply_rope(q_pe, rope)
    return jnp.concatenate([q_nope, q_pe], axis=-1)

def _mla_kv(zkv, kv_norm_g, w_ukv, rope):
    B, T = zkv.shape[:2]
    kv = (_rms_norm(zkv[..., :MLA_KV_RANK], kv_norm_g) @ w_ukv).reshape(B, T, MLA_HEADS, MLA_NOPE + MLA_V)
    k_nope, v = kv[..., :MLA_NOPE], kv[..., MLA_NOPE:]
    k_pe = zkv[..., MLA_KV_RANK:][:, :, None, :]
    if rope is not None:
        k_pe = _apply_rope(k_pe, rope)
    k = jnp.concatenate([k_nope, jnp.broadcast_to(k_pe, (B, T, MLA_HEADS, MLA_ROPE))], axis=-1)
    return k, v

def _mla_block(qb, k, v):
    s = jnp.einsum('bqhd,bkhd->bhqk', qb, k).astype(jnp.float32) * MLA_SCALE
    p = jax.nn.softmax(s, axis=-1).astype(v.dtype)
    return jnp.einsum('bhqk,bkhd->bqhd', p, v)

def _even_mixer(h, hc, rope, w_in, conv_w, q_norm_g, w_uq, kv_norm_g, w_ukv, w_out, need_ctx):
    B, T, _ = h.shape
    z = h @ w_in
    a_lat = _short_conv(z[..., :SC_IN], conv_w)
    q_lat = _mla_q(z[..., SC_IN:SC_IN + MLA_Q_RANK], q_norm_g, w_uq, rope)
    k_lat, v_lat = _mla_kv(z[..., SC_IN + MLA_Q_RANK:], kv_norm_g, w_ukv, rope)
    if need_ctx:
        zc = hc @ w_in
        k_ctx, v_ctx = _mla_kv(zc[..., SC_IN + MLA_Q_RANK:], kv_norm_g, w_ukv, None)
    else:
        k_ctx, v_ctx = _mla_kv(hc @ w_in[:, SC_IN + MLA_Q_RANK:], kv_norm_g, w_ukv, None)
    k_all = jnp.concatenate([k_ctx, k_lat], axis=1)
    v_all = jnp.concatenate([v_ctx, v_lat], axis=1)
    b_lat = _map_query_blocks(lambda qb: _mla_block(qb, k_all, v_all), q_lat)
    y = jnp.concatenate([a_lat, b_lat.reshape(B, T, -1)], axis=-1) @ w_out
    yc = None
    if need_ctx:
        L = hc.shape[1]
        a_ctx = _short_conv(zc[..., :SC_IN], conv_w)
        q_ctx = _mla_q(zc[..., SC_IN:SC_IN + MLA_Q_RANK], q_norm_g, w_uq, None)
        b_ctx = _map_query_blocks(lambda qb: _mla_block(qb, k_ctx, v_ctx), q_ctx)
        yc = jnp.concatenate([a_ctx, b_ctx.reshape(hc.shape[0], L, -1)], axis=-1) @ w_out
    return y, yc

def _diff_q(zq, rope):
    B, T = zq.shape[:2]
    q = zq.reshape(B, T, DIFF_HEADS, 2, DIFF_HEAD)
    return q if rope is None else _apply_rope(q, rope)

def _diff_kv(zkv, rope):
    B, T = zkv.shape[:2]
    k = zkv[..., :DIFF_WIDTH].reshape(B, T, DIFF_HEADS, 2, DIFF_HEAD)
    if rope is not None:
        k = _apply_rope(k, rope)
    v = zkv[..., DIFF_WIDTH:].reshape(B, T, DIFF_HEADS, 2 * DIFF_HEAD)
    return k, v

def _diff_block(qb, k, v, lam, subln_g, lam_init):
    s = jnp.einsum('bqhmd,bkhmd->bhmqk', qb, k).astype(jnp.float32) * DIFF_SCALE
    p = jax.nn.softmax(s, axis=-1)
    a = (p[:, :, 0] - lam * p[:, :, 1]).astype(v.dtype)
    o = jnp.einsum('bhqk,bkhe->bqhe', a, v)
    return _rms_norm(o, subln_g) * (1.0 - lam_init)

def _fourier(f):
    B, T, _ = f.shape
    g = f.reshape(B, T, FNET_GROUPS, FNET_GROUP_DIM).astype(jnp.float32)
    y = jnp.fft.fftn(g, axes=(1, 3), norm='ortho').real
    return y.reshape(B, T, FNET_WIDTH).astype(f.dtype)

def _odd_mixer(h, hc, rope, w_in, lam_p, subln_g, w_out, lam_init, need_ctx):
    B, T, _ = h.shape
    lp = lam_p.astype(jnp.float32)
    lam = jnp.exp(jnp.sum(lp[0] * lp[1])) - jnp.exp(jnp.sum(lp[2] * lp[3])) + lam_init
    z = h @ w_in
    q_lat = _diff_q(z[..., :DIFF_WIDTH], rope)
    k_lat, v_lat = _diff_kv(z[..., DIFF_WIDTH:3 * DIFF_WIDTH], rope)
    if need_ctx:
        zc = hc @ w_in
        k_ctx, v_ctx = _diff_kv(zc[..., DIFF_WIDTH:3 * DIFF_WIDTH], None)
    else:
        k_ctx, v_ctx = _diff_kv(hc @ w_in[:, DIFF_WIDTH:3 * DIFF_WIDTH], None)
    k_all = jnp.concatenate([k_ctx, k_lat], axis=1)
    v_all = jnp.concatenate([v_ctx, v_lat], axis=1)
    c_lat = _map_query_blocks(lambda qb: _diff_block(qb, k_all, v_all, lam, subln_g, lam_init), q_lat)
    d_lat = _fourier(z[..., 3 * DIFF_WIDTH:])
    y = jnp.concatenate([c_lat.reshape(B, T, DIFF_WIDTH), d_lat], axis=-1) @ w_out
    yc = None
    if need_ctx:
        L = hc.shape[1]
        q_ctx = _diff_q(zc[..., :DIFF_WIDTH], None)
        c_ctx_out = _map_query_blocks(lambda qb: _diff_block(qb, k_ctx, v_ctx, lam, subln_g, lam_init), q_ctx)
        d_ctx = _fourier(zc[..., 3 * DIFF_WIDTH:])
        yc = jnp.concatenate([c_ctx_out.reshape(hc.shape[0], L, DIFF_WIDTH), d_ctx], axis=-1) @ w_out
    return y, yc

def setup_inputs(seed: int = 0) -> dict:
    key = jax.random.key(seed)
    ks = iter(list(jax.random.split(key, 32)))
    ne, no = (DEPTH + 1) // 2, DEPTH // 2
    D, F, E = D_MODEL, D_FF, N_EXPERTS

    def nrm(shape, std):
        return std * jax.random.normal(next(ks), shape, jnp.float32)

    def gain(shape):
        return 1.0 + nrm(shape, 0.02)

    return {
        'x': nrm((BATCH, SEQ, D), 1.0),
        'c': nrm((BATCH, D), 1.0),
        'ctx': nrm((BATCH, CTX_LEN, D), 1.0),
        'c_ctx': nrm((D,), 1.0),
        'ev_mod_w': nrm((ne, D, N_MOD * D), 0.5 * D ** -0.5),
        'ev_mod_b': nrm((ne, N_MOD * D), 0.02),
        'ev_norm_g': gain((ne, 4, D)),
        'ev_w_in': nrm((ne, D, EVEN_IN), D ** -0.5),
        'ev_conv_w': nrm((ne, SC_KERNEL, SC_WIDTH), SC_KERNEL ** -0.5),
        'ev_q_norm_g': gain((ne, MLA_Q_RANK)),
        'ev_w_uq': nrm((ne, MLA_Q_RANK, MLA_HEADS * (MLA_NOPE + MLA_ROPE)), MLA_Q_RANK ** -0.5),
        'ev_kv_norm_g': gain((ne, MLA_KV_RANK)),
        'ev_w_ukv': nrm((ne, MLA_KV_RANK, MLA_HEADS * (MLA_NOPE + MLA_V)), MLA_KV_RANK ** -0.5),
        'ev_w_out': nrm((ne, D, D), D ** -0.5),
        'ev_ffn_gate': nrm((ne, D, F), D ** -0.5),
        'ev_ffn_up': nrm((ne, D, F), D ** -0.5),
        'ev_ffn_down': nrm((ne, F, D), F ** -0.5),
        'od_mod_w': nrm((no, D, N_MOD * D), 0.5 * D ** -0.5),
        'od_mod_b': nrm((no, N_MOD * D), 0.02),
        'od_norm_g': gain((no, 4, D)),
        'od_w_in': nrm((no, D, ODD_IN), D ** -0.5),
        'od_lambda': nrm((no, 4, DIFF_HEAD), 0.1),
        'od_subln_g': gain((no, 2 * DIFF_HEAD)),
        'od_w_out': nrm((no, D, D), D ** -0.5),
        'od_router': nrm((no, D, E), D ** -0.5),
        'od_exp_gate': nrm((no, E, D, F), D ** -0.5),
        'od_exp_up': nrm((no, E, D, F), D ** -0.5),
        'od_exp_down': nrm((no, E, F, D), F ** -0.5),
    }

def reference(x, c, ctx, c_ctx, ev_mod_w, ev_mod_b, ev_norm_g, ev_w_in, ev_conv_w, ev_q_norm_g, ev_w_uq,
              ev_kv_norm_g, ev_w_ukv, ev_w_out, ev_ffn_gate, ev_ffn_up, ev_ffn_down, od_mod_w, od_mod_b,
              od_norm_g, od_w_in, od_lambda, od_subln_g, od_w_out, od_router, od_exp_gate, od_exp_up, od_exp_down):
    rows = x.shape[1] // GRID_W
    rope_mla = _axial_rope(rows, MLA_ROPE)
    rope_diff = _axial_rope(rows, DIFF_HEAD)
    c_ctx_row = c_ctx[None, :]
    for i in range(DEPTH):
        j = i // 2
        even = i % 2 == 0
        need_ctx = i < DEPTH - 1
        if even:
            mod_w, mod_b, norm_g = ev_mod_w[j], ev_mod_b[j], ev_norm_g[j]
            ffn = lambda t: _swiglu(t, ev_ffn_gate[j], ev_ffn_up[j], ev_ffn_down[j])
        else:
            mod_w, mod_b, norm_g = od_mod_w[j], od_mod_b[j], od_norm_g[j]
            ffn = lambda t: _moe(t, od_router[j], od_exp_gate[j], od_exp_up[j], od_exp_down[j])
        sh1, sc1, g1, sh2, sc2, g2 = _ada(c, mod_w, mod_b)
        csh1, csc1, cg1, csh2, csc2, cg2 = _ada(c_ctx_row, mod_w, mod_b)
        h = _modulate(_rms_norm(x, norm_g[0]), sh1, sc1)
        hc = _modulate(_rms_norm(ctx, norm_g[0]), csh1, csc1)
        if even:
            y, yc = _even_mixer(h, hc, rope_mla, ev_w_in[j], ev_conv_w[j], ev_q_norm_g[j], ev_w_uq[j],
                                ev_kv_norm_g[j], ev_w_ukv[j], ev_w_out[j], need_ctx)
        else:
            lam_init = 0.8 - 0.6 * math.exp(-0.3 * i)
            y, yc = _odd_mixer(h, hc, rope_diff, od_w_in[j], od_lambda[j], od_subln_g[j], od_w_out[j],
                               lam_init, need_ctx)
        x = x + g1 * _rms_norm(y, norm_g[1])
        h2 = _modulate(_rms_norm(x, norm_g[2]), sh2, sc2)
        x = x + g2 * _rms_norm(ffn(h2), norm_g[3])
        if need_ctx:
            ctx = ctx + cg1 * _rms_norm(yc, norm_g[1])
            hc2 = _modulate(_rms_norm(ctx, norm_g[2]), csh2, csc2)
            ctx = ctx + cg2 * _rms_norm(ffn(hc2), norm_g[3])
    return x


_drawn_inputs = setup_inputs


def setup_inputs(seed=0):
    import zlib

    import numpy as np

    out = dict(_drawn_inputs(seed))
    spreads = {}
    factors = {'ev_q_norm_g': 4.879, 'ev_kv_norm_g': 7.227, 'od_subln_g': 4.159}
    for name, (base, spread) in spreads.items():
        noise = np.random.default_rng([zlib.crc32(name.encode()), seed]).standard_normal(out[name].shape)
        drawn = base * np.exp(spread * noise) if base else spread * noise
        out[name] = __import__('jax').numpy.asarray(drawn.astype(out[name].dtype))
    for name, factor in factors.items():
        out[name] = (out[name] * factor).astype(out[name].dtype)
    return out
```

```python
import math
from contextlib import ExitStack

import concourse.bass as bass
import numpy as np
from concourse import mybir

ALU = mybir.AluOpType
ACT = mybir.ActivationFunctionType
AX = mybir.AxisListType
F32 = mybir.dt.float32
F32R = mybir.dt.float32r
I32 = mybir.dt.int32

P = 128
D = 1024
KD = D // P
TL = 256
T = 512
FF = 2816
NF = FF // P
NE = 8
EPS = 1e-6
HEADS = 4
QR, KVR = 3, 2
MLA_SCALE = (128 + 64) ** -0.5
DH = 6
DIFF_SCALE = 64 ** -0.5
LAM_INIT = 0.8 - 0.6 * math.exp(-0.3)

PIECE = 2048
P_MOD_A = 0
P_WIN = 8
P_MOD_B = 17
P_MOD_O = 33
P_WOUT = 57
P_MOE = 108
PER_EXPERT = 33
MOE_PIECES = NE * PER_EXPERT
EARLY_SLOTS = 3
SLOTS = 11
SPLITS = 3
AHEAD = SPLITS
S_WIN, S_WOUT, S_GU, S_DOWN, S_OIN, S_OOUT, S_MOE = 0, 9, 13, 35, 46, 56, 60


def piece_of(s):
    return P_WIN + s if s < S_WOUT else P_WOUT + s - S_WOUT


VEC = {}
_at = 0
for _n, _w in (("cond", 16), ("mod_b0", 96), ("mod_b1", 96), ("norm0", 64), ("norm1", 64), ("conv", 12),
               ("qn", QR), ("kvn", KVR), ("subln", 1), ("lam", 4), ("router", 64)):
    VEC[_n] = (_at, _w)
    _at += _w
NVEC = _at

NORMS = [(KD, T), (QR, T), (KVR, T), (KD, T), (KD, T), (KD, T), (KD, T), (KD, TL), (KD, TL), (KD, TL)]
N_E1, N_Q, N_KV, N_EY, N_E2, N_EF, N_O1, N_OY, N_O2, N_OF = range(10)
NDIM = [D, QR * P, KVR * P] + [D] * 7


def chunks_before(n):
    return sum(k for k, _ in NORMS[:n])


RES_BEFORE = {N_E1: 0, N_EY: 0, N_E2: 2 * KD, N_EF: 2 * KD, N_O1: 4 * KD, N_OY: 4 * KD, N_O2: 5 * KD, N_OF: 5 * KD}


def expert_order():
    order = [("gu", 0, 0), ("gu", 0, 1)]
    for g in range(1, 11):
        order += [("gu", g, 0), ("gu", g, 1), ("d", g - 1, 0)]
    return order + [("d", 10, 0)]


ORDER = expert_order()


def build(nc, x_d, vec_d, cst_d, rope_d, dft_d, uq_d, ukv_d, w_d, out_d):
    with ExitStack() as ctx:
        def sb(name, shape, dt=F32):
            return ctx.enter_context(nc.sbuf_tensor(name, shape, dt))

        sems = {}

        def sem(name):
            if name not in sems:
                sems[name] = ctx.enter_context(nc.semaphore(name))
            return sems[name]

        ps = ctx.enter_context(nc.psum_tensor("ps", [P, 8, 512], F32))
        raw = sb("raw", [P, SLOTS * PIECE])
        wh = sb("wh", [P, SPLITS, PIECE], F32R)
        wl = sb("wl", [P, SPLITS, PIECE], F32R)
        ah = sb("ah", [P, KD, T], F32R)
        al = sb("al", [P, KD, T], F32R)
        sh = sb("sh", [P, 2, T], F32R)
        sl = sb("sl", [P, 2, T], F32R)
        x = sb("x", [P, KD, T])
        cst = sb("cst", [P, 5, P])
        ident, ones, tri, iota, rot = (cst[:, i, :] for i in range(5))
        rope = sb("rope", [P, 2, TL])
        vec = sb("vec", [P, NVEC])
        condS = vec[:, VEC["cond"][0]:VEC["cond"][0] + 16].rearrange("p (k c) -> p k c", k=KD)
        mod0 = sb("mod0", [P, 48, 2])
        mod1 = sb("mod1", [P, 48, 2])
        scl = sb("scl", [P, 2, 4, KD, 2])
        rinv = sb("rinv", [P, T])
        sq = sb("sq", [P, 2, T])
        t2 = sb("t2", [P, T])
        eps = sb("eps", [P, 1])
        small = sb("small", [P, 96])
        cnt = sb("cnt", [P, 1], I32)
        rg = rope[:, 0, 0:4 * (NE + 1)].rearrange("p (e c) -> p e c", c=4)
        cur = rope[:, 1, 0:4]
        sel = sh[:, 1, 256:512].rearrange("p (t s) -> p t s", t=2)
        selT = sh[:, 0, 256:512]
        gslot = rope[:, 1, 8:9]

        H0 = EARLY_SLOTS * PIECE

        def area(at, *dims):
            n = int(np.prod(dims))
            v = raw[:, H0 + at:H0 + at + n]
            if len(dims) == 2:
                v = v.rearrange("p (a b) -> p a b", a=dims[0])
            if len(dims) == 3:
                v = v.rearrange("p (a b c) -> p a b c", a=dims[0], b=dims[1])
            return v

        t3 = area(15872, T)
        tmp = [t2[:, :], t3]
        b_gate = area(0, HEADS, T)
        q_nope = area(0, HEADS, T)
        q_pe = area(2048, HEADS, T)
        cu = area(4096, HEADS * 2, 258).rearrange("p (c s) t -> p c s t", s=2)
        k_nope = area(4096, HEADS, T)
        v_e = area(6160, 4, T)
        uq = area(8208, QR, 768)
        ukv = area(10512, KVR, 1024)
        zq = area(12560, QR, T)
        zkv = area(14096, KVR, T)
        k_pe = area(15120, T)
        pr_e = area(12560, 2, T)
        pt_e = area(13584, 2, T)
        y_e = area(0, KD, T)
        hid = area(0, NF, T)
        y2_e = area(11264, KD, T)
        q_o = area(0, DH, TL)
        k_o = area(1536, DH, T)
        v_o = area(4608, 4, 768)
        f_o = area(7680, 2, TL)
        mid = area(8192, 4, 256)
        dftc = area(9216, 256)
        dftt = area(9472, 4, 256)
        o_o = area(10496, DH, TL)
        pr_o = area(12032, 2, 2, T)
        pt_o = area(14080, 2, T)
        o_sq = area(12032, DH, TL)
        o_rinv = area(13568, DH, TL)
        y_o = area(0, KD, TL)
        h2f = area(2048, KD, TL)
        h2h, h2l = (a[:, 0:4, :].rearrange("p a b -> p (a b)").rearrange("p (t f) -> p t f", t=2) for a in (ah, al))
        xeh, xel = (a[:, 4:6, :].rearrange("p a b -> p (a b)").rearrange("p (k s) -> p k s", k=KD) for a in (ah, al))
        yh, yl = (a[:, 6:8, :].rearrange("p a b -> p (a b)") for a in (ah, al))
        acc = x[:, :, TL:T]
        silu_t = lambda g: sq[:, 0, (g % 2) * 256:(g % 2 + 1) * 256]
        hh = lambda g: sq[:, 1, (g % 2) * 256:(g % 2 + 1) * 256]

        def vc(name, a=0, b=None):
            o, w = VEC[name]
            return vec[:, o + a:o + (w if b is None else b)]

        vecs_loaded, x_loaded, even_loaded, odd_loaded = map(sem, ("vecs_loaded", "x_loaded", "even_loaded", "odd_loaded"))
        landed = [sem(f"landed{i}") for i in range(SLOTS)]
        mod_used, w_hi, w_lo, w_used = map(sem, ("mod_used", "w_hi", "w_lo", "w_used"))
        evac_act, evac_dve = sem("evac_act"), sem("evac_dve")
        sq_ready, ssq_done, root_ready, rinv_ready, t_ready = map(
            sem, ("sq_ready", "ssq_done", "root_ready", "rinv_ready", "t_ready"))
        mod_h, mod_hi, mod_lo, res_done = map(sem, ("mod_h", "mod_hi", "mod_lo", "res_done"))
        consts_set = sem("consts_set")
        cond_ready, modv_ready, scales_ready = map(sem, ("cond_ready", "modv_ready", "scales_ready"))

        evac_by = (["act"] * 2 + ["dve"] * 4 + ["act"] * 3 + ["act"] * 4 + ["dve"] * 22 + ["act"] * 10 + ["act"] * 4)

        def ordinal(s):
            return s if s < S_DOWN else s - (S_OIN - S_DOWN)

        def evacs(s, who):
            return sum(w == who for w in evac_by[:ordinal(s) + 1])

        def slot_of(i):
            return i % EARLY_SLOTS if i < P_MOE else (i - P_MOE) % SLOTS

        def landings(i):
            return i // EARLY_SLOTS + 1

        early_landings = [P_MOE // EARLY_SLOTS] * EARLY_SLOTS + [0] * (SLOTS - EARLY_SLOTS)

        def slot(n):
            return raw[:, n * PIECE:(n + 1) * PIECE]

        block = ctx.enter_context(nc.Block())
        NK = chunks_before(len(NORMS))

        @block.sync
        def _(sp):
            sp.dma_start(vec[:, :], vec_d).then_inc(vecs_loaded, 16)
            sp.dma_start(x[:, :, :], x_d).then_inc(x_loaded, 16)
            sp.dma_start(cst[:, :, :], cst_d).then_inc(sem("cst_loaded"), 16)
            sp.dma_start(rope[:, :, :], rope_d).then_inc(sem("rope_loaded"), 16)
            sp.dma_start(uq, uq_d).then_inc(sem("uq_loaded"), 16)
            sp.dma_start(ukv, ukv_d).then_inc(sem("ukv_loaded"), 16)
            split_index = {piece_of(s): s for s in range(S_MOE)}
            for i in range(P_MOE):
                if i == piece_of(S_OIN) + 5:
                    sp.wait_ge(sem("y2_used"), 1)
                    sp.dma_start(dftc, dft_d[:, 0:256]).then_inc(sem("dftc_loaded"), 16)
                    sp.dma_start(dftt, dft_d[:, 256:1280].rearrange("p (a b) -> p a b", a=4)).then_inc(sem("dftt_loaded"), 16)
                if i >= EARLY_SLOTS:
                    last = i - EARLY_SLOTS
                    if last in split_index:
                        sp.wait_ge(w_lo, split_index[last] + 1)
                    else:
                        sp.wait_ge(mod_used, last + 1 if last < P_WIN else last + 1 - 9)
                sp.dma_start(slot(slot_of(i)), w_d[i]).then_inc(landed[slot_of(i)], 16)

            for j in range(SLOTS):
                if j < EARLY_SLOTS:
                    sp.wait_ge(w_lo, S_MOE - EARLY_SLOTS + j + 1)
                if j == EARLY_SLOTS:
                    sp.wait_ge(sem("tok_lo"), 2)
                sp.dma_start(slot(j), w_d[P_MOE + j]).then_inc(landed[j], 16)
            with sp.Fori(0, NE - 1) as e:
                for r in range(PER_EXPERT):
                    sp.wait_ge(w_lo, S_MOE + PER_EXPERT * e + r + 1)
                    sp.dma_start(slot(r % SLOTS), w_d[bass.ds(PER_EXPERT * e + (P_MOE + SLOTS + r), 1)].rearrange("o p n -> (o p) n")
                                 ).then_inc(landed[r % SLOTS], 16)
            for j in range(PER_EXPERT * (NE - 1) + SLOTS, MOE_PIECES + AHEAD):
                sp.wait_ge(w_lo, S_MOE + j - SLOTS + 1)
                sp.dma_start(slot(j % SLOTS), w_d[P_MOE + j]).then_inc(landed[j % SLOTS], 16)
            sp.wait_ge(sem("count_ready"), 1)
            most = sp.value_load(cnt[0:1, 0:1], min_val=0, max_val=TL)
            with sp.If(most > P):
                with sp.Fori(0, NE) as e:
                    for r in range(AHEAD, PER_EXPERT + AHEAD):
                        sp.wait_ge(w_lo, S_MOE + MOE_PIECES - SLOTS + r + 1 + PER_EXPERT * e)
                        sp.dma_start(slot(r % SLOTS), w_d[bass.ds(PER_EXPERT * e + (P_MOE + r), 1)].rearrange("o p n -> (o p) n")
                                     ).then_inc(landed[r % SLOTS], 16)
            for k in range(KD):
                sp.wait_ge(res_done, RES_BEFORE[N_OF] + k + 1)
                sp.dma_start(out_d[:, k, :], x[:, k, 0:TL]).then_inc(sem("stored"), 16)
            sp.wait_ge(sem("stored"), 16 * KD)

        @block.scalar
        def _(act):
            chain = [0]

            def link(ins):
                chain[0] += 1
                ins.then_inc(sem("act_chain"), 1)
                act.wait_ge(sem("act_chain"), chain[0])

            done = [0]

            def split(upto):
                while done[0] <= min(upto, S_MOE - 1):
                    s = done[0]
                    i = piece_of(s)
                    act.wait_ge(landed[slot_of(i)], 16 * landings(i))
                    if s >= SPLITS:
                        act.wait_ge(w_used, s - SPLITS + 1)
                    act.activation(wh[:, s % SPLITS, :], slot(slot_of(i)), ACT.Copy).then_inc(w_hi, 1)
                    done[0] += 1

            def squares(n, src, ready=None):
                K, W = NORMS[n]
                for k in range(K):
                    j = chunks_before(n) + k
                    if j >= 2:
                        act.wait_ge(ssq_done, j - 1)
                    if ready:
                        ready(k)
                    act.activation(sq[:, j % 2, 0:W], src(k), ACT.Square).then_inc(sq_ready, 1)

            def root(n):
                K, W = NORMS[n]
                act.wait_ge(ssq_done, chunks_before(n) + K)
                if n:
                    act.wait_ge(t_ready, chunks_before(n))
                act.activation(rinv[:, 0:W], ps[:, 4, 0:W], ACT.Sqrt, bias=eps[:, 0:1], scale=1.0 / NDIM[n]).then_inc(root_ready, 1)

            def modulate(n, m, layer, which, shift, dst=None):
                K, W = NORMS[n]
                modv = (mod0, mod1)[layer]
                for k in range(K):
                    j = chunks_before(n) + k
                    act.wait_ge(t_ready, j + 1)
                    b = tmp[j % 2] if dst is None else dst(k)
                    for c in range(W // TL):
                        act.activation(b[:, c * TL:(c + 1) * TL], b[:, c * TL:(c + 1) * TL], ACT.Identity,
                                       bias=modv[:, shift + k, c:c + 1],
                                       scale=scl[:, layer, which, k, c:c + 1]).then_inc(mod_h, 1)
                    if dst is None:
                        act.wait_ge(mod_h, 2 * (KD * m + k + 1))
                        act.activation(ah[:, k, 0:W], b[:, 0:W], ACT.Copy).then_inc(mod_hi, 1)

            act.wait_ge(vecs_loaded, 16)
            act.activation(vc("cond"), vc("cond"), ACT.Silu).then_inc(cond_ready, 1)
            act.wait_ge(x_loaded, 16)
            squares(N_E1, lambda k: x[:, k, :])
            act.wait_ge(sem("lam_sums"), 1)
            act.activation(small[:, 2:4], ps[:, 5, 0:2], ACT.Exp).then_inc(sem("lam_exp"), 1)
            act.wait_ge(consts_set, 1)
            root(N_E1)
            act.wait_ge(scales_ready, 1)
            modulate(N_E1, 0, 0, 0, 0)

            split(2)
            for p in range(9):
                split(min(p + 2, S_WOUT - 1))
                if evac_by[p] == "dve":
                    continue
                act.wait_ge(w_used, p + 1)
                bank = 2 * (p % 2)
                dst = {0: (b_gate[:, 0, :], b_gate[:, 1, :]), 1: (b_gate[:, 2, :], b_gate[:, 3, :]),
                       6: (zq[:, 0, :], zq[:, 1, :]), 7: (zq[:, 2, :], zkv[:, 0, :]),
                       8: (zkv[:, 1, :], k_pe[0:64, :])}[p]
                n = 64 if p == 8 else P
                act.activation(dst[0], ps[:, bank, :], ACT.Copy)
                act.activation(dst[1], ps[0:n, bank + 1, :], ACT.Copy).then_inc(evac_act, 1)
            act.wait_ge(evac_act, evacs(S_WIN + 8, "act"))
            squares(N_Q, lambda k: zq[:, k, :])
            squares(N_KV, lambda k: zkv[:, k, :])
            root(N_Q)
            for c in range(HEADS):
                act.wait_ge(sem("conv_ready"), c + 1)
                act.activation(ah[:, c, :], tmp[c % 2], ACT.Copy).then_inc(sem("conv_hi"), 1)
                if c == 1:
                    root(N_KV)

            dsts = ([(q_nope[:, h, :], P) for h in range(HEADS)] + [(q_pe[0:64, h, :], 64) for h in range(HEADS)]
                    + [(k_nope[:, h, :], P) for h in range(HEADS)] + [(v_e[:, t, :], P) for t in range(4)])
            for n, (dst, w) in enumerate(dsts):
                act.wait_ge(sem("proj_ps"), n + 1)
                act.activation(dst, ps[0:w, n % 4, :], ACT.Copy).then_inc(sem("proj_ready"), 1)

            def attention(name, units, exp, out):
                s_ = lambda k: sem(f"{name}_{k}")
                for i in range(len(units) + 2):
                    if i < len(units):
                        act.wait_ge(s_("negmax"), i + 1)
                        if i >= 2:
                            act.wait_ge(s_("turned"), i - 1)
                        exp(i).then_inc(s_("exp"), 1)
                    if 1 <= i <= len(units):
                        u = i - 1
                        n = units[u][2]
                        act.wait_ge(s_("turned"), u + 1)
                        if u >= 2:
                            act.wait_ge(s_("pv"), u - 1)
                        pt, bank = (pt_e, 2) if name == "mla" else (pt_o, 4)
                        act.activation(pt[:, u % 2, 0:n], ps[:, bank + u % 2, 0:n], ACT.Copy).then_inc(s_("pt"), 1)
                    if i >= 2:
                        act.wait_ge(s_("pv"), i - 1)
                        out(i - 2)

            units = mla_units()

            def exp_e(i):
                n = units[i][2]
                return act.activation(pr_e[:, i % 2, 0:n], ps[:, i % 2, 0:n], ACT.Exp, bias=small[:, 16 + i:17 + i],
                                      scale=MLA_SCALE, accum_out=small[:, 32 + i:33 + i])

            def out_e(u):
                h, j, _, _ = units[u]
                act.activation(ah[:, HEADS + h, j * P:(j + 1) * P], ps[:, 4 + u % 2, 0:P], ACT.Copy
                               ).then_inc(sem("mla_ohi"), 1)

            attention("mla", units, exp_e, out_e)

            for p in range(4):
                s = S_WOUT + p
                split(s + 2)
                act.wait_ge(w_used, s + 1)
                bank = 2 * (ordinal(s) % 2)
                act.activation(y_e[:, 2 * p:2 * p + 2, :], ps[:, bank:bank + 2, :], ACT.Copy).then_inc(evac_act, 1)
            for p in range(4):
                act.wait_ge(evac_act, evacs(S_WOUT + p, "act"))
            squares(N_EY, lambda k: y_e[:, k, :])
            root(N_EY)
            squares(N_E2, lambda k: x[:, k, :], lambda k: act.wait_ge(res_done, 2 * (k + 1)))
            root(N_E2)
            modulate(N_E2, 1, 0, 2, 24)

            for m in range(NF):
                s = S_GU + m
                split(s + 2)
                act.wait_ge(w_used, s + 1)
                if m >= 2:
                    act.wait_ge(evac_dve, evacs(s - 2, "dve"))
                act.activation(tmp[m % 2], ps[:, 2 * (ordinal(s) % 2), :], ACT.Silu).then_inc(sem("silu"), 1)

            def hidden_hi(f):
                if f >= 2:
                    if f % 2 == 0:
                        act.wait_ge(sem("f_used"), f // 2)
                    else:
                        act.wait_ge(w_used, S_DOWN + (f - 1) // 2)
                act.wait_ge(evac_dve, evacs(S_GU + f, "dve"))
                act.activation(sh[:, f % 2, :], hid[:, f, :], ACT.Copy).then_inc(sem("hid_hi"), 1)

            hidden_hi(0)
            hidden_hi(1)
            for d in range(NF // 2):
                split(S_DOWN + d + 2)
                if d + 1 < NF // 2:
                    hidden_hi(2 * d + 2)
                    hidden_hi(2 * d + 3)
            act.wait_ge(w_used, S_DOWN + NF // 2)
            act.wait_ge(sem("hid_lo"), NF)
            for q in range(2):
                act.activation(y2_e[:, 2 * q:2 * q + 2, :], ps[:, 2 * q:2 * q + 2, :], ACT.Copy).then_inc(sem("y2_act"), 1)
            act.wait_ge(sem("y2_act"), 2)
            act.wait_ge(sem("y2_dve"), 2)
            squares(N_EF, lambda k: y2_e[:, k, :])
            root(N_EF)
            squares(N_O1, lambda k: x[:, k, :], lambda k: act.wait_ge(res_done, 2 * KD + 2 * (k + 1)))
            root(N_O1)
            modulate(N_O1, 2, 1, 0, 0)

            for p in range(10):
                s = S_OIN + p
                split(s + 2)
                act.wait_ge(w_used, s + 1)
                bank = 2 * (ordinal(s) % 2)
                if p == 9:
                    act.activation(f_o[:, :, :], ps[:, bank:bank + 2, 0:TL], ACT.Copy).then_inc(evac_act, 1)
                elif p >= 6:
                    c = (p - 6) * 256
                    act.activation(v_o[:, :, c:c + 256],
                                   ps[:, bank:bank + 2, :].rearrange("p b (t n) -> p (b t) n", t=2),
                                   ACT.Copy).then_inc(evac_act, 1)
                elif p >= 3:
                    act.activation(k_o[:, 2 * p - 6:2 * p - 4, :], ps[:, bank:bank + 2, :], ACT.Copy).then_inc(evac_act, 1)
                else:
                    act.activation(q_o[:, 2 * p:2 * p + 2, :], ps[:, bank:bank + 2, 0:TL], ACT.Copy).then_inc(evac_act, 1)
            act.wait_ge(sem("four_ps"), 1)
            act.activation(mid[:, :, :].rearrange("p a b -> p (a b)"),
                           ps[:, 0:2, :].rearrange("p a b -> p (a b)"), ACT.Copy).then_inc(sem("four_mid"), 1)
            act.wait_ge(sem("four_ps"), 2)
            act.activation(ah[:, 6:8, 0:TL], ps[:, 2, :].rearrange("p (a b) -> p a b", a=2), ACT.Copy
                           ).then_inc(sem("four_hi"), 1)

            ounits = diff_units()

            def exp_o(i):
                for m in range(2):
                    ins = act.activation(pr_o[:, i % 2, m, :], ps[:, 2 * (i % 2) + m, :], ACT.Exp,
                                         bias=small[:, 16 + 2 * i + m:17 + 2 * i + m], scale=DIFF_SCALE,
                                         accum_out=small[:, 40 + 2 * i + m:41 + 2 * i + m])
                return ins

            def out_o(u):
                h, j, _, _ = ounits[u]
                act.activation(o_o[:, h, j * P:(j + 1) * P], ps[:, 6 + u % 2, 0:P], ACT.Copy).then_inc(sem("diff_out"), 1)

            attention("diff", ounits, exp_o, out_o)
            act.wait_ge(sem("diff_out"), len(ounits))
            act.activation(o_sq[:, :, :].rearrange("p a b -> p (a b)"), o_o[:, :, :].rearrange("p a b -> p (a b)"),
                           ACT.Square).then_inc(sem("osq_ready"), 1)
            act.wait_ge(sem("ossq_done"), 3)
            act.activation(o_rinv[:, :, :].rearrange("p a b -> p (a b)"),
                           ps[:, 0:3, :].rearrange("p a b -> p (a b)"), ACT.Sqrt, bias=eps[:, 0:1],
                           scale=1.0 / P).then_inc(sem("oroot"), 1)
            for h in range(DH):
                act.wait_ge(sem("o_ready"), h + 1)
                act.activation(ah[:, h, 0:TL], o_o[:, h, :], ACT.Copy).then_inc(sem("o_hi"), 1)

            for p in range(4):
                s = S_OOUT + p
                split(s + 2)
                act.wait_ge(w_used, s + 1)
                bank = 2 * (ordinal(s) % 2)
                act.activation(y_o[:, 2 * p:2 * p + 2, :], ps[:, bank:bank + 2, 0:TL], ACT.Copy).then_inc(evac_act, 1)
            act.wait_ge(evac_act, evacs(S_OOUT + 3, "act"))
            squares(N_OY, lambda k: y_o[:, k, :])
            root(N_OY)
            squares(N_O2, lambda k: x[:, k, 0:TL], lambda k: act.wait_ge(res_done, 4 * KD + k + 1))
            root(N_O2)
            modulate(N_O2, 3, 1, 2, 24, lambda k: h2f[:, k, :])

            act.wait_ge(sem("top_diff"), 1)
            act.activation(small[:, 4:6], small[:, 2:4], ACT.Exp).then_inc(sem("top_exp"), 1)
            for t in range(2):
                act.wait_ge(sem("tok_ps"), t + 1)
                act.activation(h2h[:, t, :], ps[:, 2 * t:2 * t + 2, :].rearrange("p a b -> p (a b)"), ACT.Copy
                               ).then_inc(sem("tok_hi"), 1)

            def gathered(idx):
                act.wait_ge(sem("xh_ps"), idx)
                act.activation(xeh[:, :, :].rearrange("p a b -> p (a b)"),
                               ps[:, 5:7, :].rearrange("p a b -> p (a b)"), ACT.Copy).then_inc(sem("xe_h"), 1)

            def experts(ps_no):
                base, gb, ab = S_MOE + MOE_PIECES * ps_no, 88 * ps_no, 9 * ps_no

                def split_q(e, q):
                    n = q % SLOTS
                    act.wait_ge(landed[n], 3 * 16 * e + 16 * (early_landings[n] + 24 * ps_no + q // SLOTS + 1))
                    act.wait_ge(w_used, PER_EXPERT * e + base + q - SPLITS + 1)
                    act.activation(wh[:, q % SPLITS, :], slot(n), ACT.Copy).then_inc(w_hi, 1)

                if ps_no == 0:
                    for q in range(AHEAD):
                        split_q(0, q)
                gathered(ab + 1)
                with act.Fori(0, NE) as e:
                    for q, (kind, g, half) in enumerate(ORDER):
                        if kind == "gu" and half == 1:
                            act.wait_ge(w_used, PER_EXPERT * e + base + q + 1)
                            gu = ps[:, g % 2, :].rearrange("p (b w c) -> p b w c", b=2, w=2)
                            act.activation(silu_t(g).rearrange("p (b c) -> p b c", b=2), gu[:, :, 0, :],
                                           ACT.Silu).then_inc(sem("moe_silu"), 1)
                        if q == 32:
                            act.wait_ge(w_used, PER_EXPERT * e + base + PER_EXPERT)
                            act.activation(yh, ps[:, 2:4, :].rearrange("p a b -> p (a b)"), ACT.Copy,
                                           scale=gslot).then_inc(sem("y_h"), 1)
                        split_q(e, q + AHEAD)
                        turned = {3: 0, 4: 1}.get(q, g + 1 if kind == "d" and 1 <= g <= 9 else None)
                        if turned is not None:
                            act.wait_ge(sem("hid_T"), 11 * e + (gb + turned + 1))
                            act.activation(sh[:, turned % 2, 0:256], ps[:, 4, 0:256], ACT.Copy).then_inc(sem("hT_hi"), 1)
                        if q == 4:
                            act.wait_ge(sem("selT_ps"), e + (8 * ps_no + 1))
                            act.activation(selT, ps[:, 7, 0:TL], ACT.Copy)
                            act.activation(gslot, ps[:, 7, TL:TL + 1], ACT.Copy).then_inc(sem("selT_ready"), 1)
                        if q == 31:
                            gathered(e + (ab + 2))

            experts(0)
            act.wait_ge(sem("count_ready"), 1)
            most = act.value_load(cnt[0:1, 0:1], min_val=0, max_val=TL)
            with act.If(most > P):
                experts(1)
            squares(N_OF, lambda k: acc[:, k, :], lambda k: act.wait_ge(sem("acc_final"), 1))
            root(N_OF)

        @block.vector
        def _(dve):
            chain = [0]

            def link(ins):
                chain[0] += 1
                ins.then_inc(sem("dve_chain"), 1)
                dve.wait_ge(sem("dve_chain"), chain[0])

            done = [0]

            def split(upto):
                while done[0] <= min(upto, S_MOE - 1):
                    s = done[0]
                    dve.wait_ge(w_hi, s + 1)
                    dve.tensor_tensor(wl[:, s % SPLITS, :], slot(slot_of(piece_of(s))), wh[:, s % SPLITS, :].bitcast(F32),
                                      ALU.subtract).then_inc(w_lo, 1)
                    done[0] += 1

            def inverse(n):
                W = NORMS[n][1]
                dve.wait_ge(root_ready, n + 1)
                dve.reciprocal(rinv[:, 0:W], rinv[:, 0:W]).then_inc(rinv_ready, 1)
                dve.wait_ge(rinv_ready, n + 1)

            def normed(n, src, dst, k):
                dve.tensor_tensor(dst, src, rinv[:, 0:NORMS[n][1]], ALU.mult).then_inc(t_ready, 1)

            def modulate(n, m, dst=None):
                K, W = NORMS[n]
                inverse(n)
                dve.wait_ge(res_done, RES_BEFORE[n])
                for k in range(K + 1):
                    if k < K:
                        j = chunks_before(n) + k
                        if k >= 2 and dst is None:
                            dve.wait_ge(mod_lo, KD * m + k - 1)
                        normed(n, x[:, k, 0:W], tmp[j % 2] if dst is None else dst(k), k)
                    if k and dst is None:
                        j = chunks_before(n) + k - 1
                        dve.wait_ge(mod_hi, KD * m + k)
                        dve.tensor_tensor(al[:, k - 1, 0:W], tmp[j % 2][:, 0:W], ah[:, k - 1, 0:W].bitcast(F32),
                                          ALU.subtract).then_inc(mod_lo, 1)

            def residual(n, src, layer, which):
                K, W = NORMS[n]
                inverse(n)
                for k in range(K + 1):
                    if k < K:
                        j = chunks_before(n) + k
                        if k >= 2:
                            dve.wait_ge(res_done, RES_BEFORE[n] + (W // TL) * (k - 1))
                        normed(n, src(k), tmp[j % 2][:, 0:W], k)
                    if k:
                        j = chunks_before(n) + k - 1
                        dve.wait_ge(t_ready, j + 1)
                        for c in range(W // TL):
                            dve.scalar_tensor_tensor(
                                out=x[:, k - 1, c * TL:(c + 1) * TL], in0=tmp[j % 2][:, c * TL:(c + 1) * TL],
                                scalar=scl[:, layer, which, k - 1, c:c + 1], in1=x[:, k - 1, c * TL:(c + 1) * TL],
                                op0=ALU.mult, op1=ALU.add).then_inc(res_done, 1)

            def flat(v):
                return v.rearrange("p a b -> p (a b)")

            def take_modulation(layer, lo, hi, bank):
                modv = (mod0, mod1)[layer]
                link(dve.tensor_tensor(flat(modv[:, lo:hi, :]), ps[:, bank, 2 * lo:2 * hi],
                                       vc(f"mod_b{layer}", 2 * lo, 2 * hi), ALU.add))

            def scale_pre(layer, which, chunk):
                modv = (mod0, mod1)[layer]
                return dve.scalar_tensor_tensor(out=flat(scl[:, layer, which, :, :]), in0=flat(modv[:, chunk:chunk + KD, :]),
                                                scalar=1.0, in1=vc(f"norm{layer}", 16 * which, 16 * which + 16),
                                                op0=ALU.add, op1=ALU.mult)

            def scale_post(layer, which, chunk):
                modv = (mod0, mod1)[layer]
                return dve.tensor_tensor(flat(scl[:, layer, which, :, :]), flat(modv[:, chunk:chunk + KD, :]),
                                         vc(f"norm{layer}", 16 * which, 16 * which + 16), ALU.mult)

            dve.memset(eps[:, :], EPS).then_inc(consts_set, 1)
            link(dve.memset(flat(area(4096, HEADS * 2, 258)), 0.0))
            dve.wait_ge(vecs_loaded, 16)
            lam = vc("lam").rearrange("p (a b) -> p a b", b=2)
            dve.tensor_tensor(small[0:64, 0:2], lam[0:64, :, 0], lam[0:64, :, 1], ALU.mult).then_inc(sem("lam_prod"), 1)
            dve.wait_ge(sem("lam_exp"), 1)
            link(dve.tensor_tensor(small[:, 6:7], small[:, 3:4], small[:, 2:3], ALU.subtract))
            link(dve.tensor_scalar(small[:, 7:8], small[:, 6:7], -LAM_INIT, None, ALU.add))
            link(dve.tensor_scalar(small[:, 8:9], vc("subln"), 1.0 - LAM_INIT, None, ALU.mult))
            dve.wait_ge(mod_used, P_WIN)
            take_modulation(0, 0, 16, 7)
            scale_pre(0, 0, 8).then_inc(scales_ready, 1)
            modulate(N_E1, 0)

            for p in range(9):
                split(min(p + 2, S_WOUT - 1))
                if evac_by[p] == "act":
                    continue
                dve.wait_ge(w_used, p + 1)
                if p >= 4:
                    dve.wait_ge(evac_dve, p - 3)
                else:
                    dve.wait_ge(mod_lo, KD)
                bank = 2 * (p % 2)
                dve.tensor_copy(tmp[p % 2], ps[:, bank, :]).then_inc(sem("c_copied"), 1)
                dve.wait_ge(sem("c_copied"), p - 1)
                dve.tensor_tensor(cu[:, p - 2, :, 1:257], ps[:, bank + 1, :].rearrange("p (s t) -> p s t", s=2),
                                  tmp[p % 2].rearrange("p (s t) -> p s t", s=2), ALU.mult).then_inc(evac_dve, 1)
            inverse(N_Q)
            dve.wait_ge(evac_act, evacs(S_WIN + 8, "act"))
            for k in range(QR):
                dve.scalar_tensor_tensor(out=zq[:, k, :], in0=zq[:, k, :], scalar=vc("qn", k, k + 1), in1=rinv[:, :],
                                         op0=ALU.mult, op1=ALU.mult).then_inc(t_ready, 1)
            dve.wait_ge(w_used, S_WIN + 9)
            dve.wait_ge(evac_dve, evacs(S_WIN + 8, "dve"))

            def conv(c):
                t = tmp[c % 2].rearrange("p (s t) -> p s t", s=2)
                w = lambda j: vc("conv", 4 * j + c, 4 * j + c + 1)
                if c >= 2:
                    dve.wait_ge(sem("conv_lo"), c - 1)
                link(dve.tensor_scalar(t, cu[:, c, :, 1:257], w(1), None, ALU.mult))
                for j in (0, 2):
                    link(dve.scalar_tensor_tensor(out=t, in0=cu[:, c, :, j:j + 256], scalar=w(j), in1=t,
                                                  op0=ALU.mult, op1=ALU.add))
                dve.tensor_tensor(tmp[c % 2], tmp[c % 2], b_gate[:, c, :], ALU.mult).then_inc(sem("conv_ready"), 1)

            def conv_lo(c):
                dve.wait_ge(sem("conv_hi"), c + 1)
                dve.tensor_tensor(al[:, c, :], tmp[c % 2], ah[:, c, :].bitcast(F32), ALU.subtract).then_inc(sem("conv_lo"), 1)

            conv(0)
            conv(1)
            inverse(N_KV)
            for k in range(KVR):
                dve.scalar_tensor_tensor(out=zkv[:, k, :], in0=zkv[:, k, :], scalar=vc("kvn", k, k + 1), in1=rinv[:, :],
                                         op0=ALU.mult, op1=ALU.mult).then_inc(t_ready, 1)
            conv_lo(0)
            conv(2)
            conv_lo(1)
            conv(3)
            conv_lo(2)
            conv_lo(3)
            dve.wait_ge(mod_used, P_WIN + 16)
            take_modulation(0, 16, 48, 7)
            link(scale_post(0, 1, 16))
            link(scale_pre(0, 2, 32))
            scale_post(0, 3, 40).then_inc(scales_ready, 1)

            cosb, sinb = rope[:, 0, :], rope[:, 1, :]

            def rotate(dst, turned, w, signal, buf, heads):
                t = tmp[buf][0:w, 0:heads * TL].rearrange("p (h t) -> p h t", h=heads)
                for h in range(heads):
                    dve.tensor_tensor(t[:, h, :], turned[:, h, :], sinb[0:w, :], ALU.mult)
                    ins = dve.tensor_tensor(dst[:, h, :], dst[:, h, :], cosb[0:w, :], ALU.mult)
                link(ins)
                dve.tensor_tensor(dst, dst, t, ALU.add).then_inc(signal, 1)

            dve.wait_ge(sem("rope_loaded"), 16)
            dve.wait_ge(sem("rope_ps"), 1)
            rotate(k_pe[0:64, None, 0:TL], ps[0:64, 5, None, 0:TL], 64, sem("rope_done"), 0, 1)
            for g in range(2):
                dve.wait_ge(sem("rope_ps"), g + 2)
                rotate(q_pe[0:64, 2 * g:2 * g + 2, 0:TL], ps[0:64, 6 + g, :].rearrange("p (h t) -> p h t", h=2), 64,
                       sem("rope_done"), 1 - g, 2)

            def attention(name, units, scale, scaled, out):
                s_ = lambda k: sem(f"{name}_{k}")
                nm = 1 if name == "mla" else 2
                sums = 32 if name == "mla" else 40
                for i in range(len(units) + 2):
                    if i < len(units):
                        n = units[i][2]
                        dve.wait_ge(s_("scores"), i + 1)
                        cols = slice(16 + nm * i, 16 + nm * (i + 1))
                        if nm == 1:
                            src = ps[:, i % 2, 0:n]
                        else:
                            src = ps[:, 2 * (i % 2):2 * (i % 2) + 2, :]
                        link(dve.tensor_reduce(small[:, cols], src, AX.X, ALU.max))
                        dve.tensor_scalar(small[:, cols], small[:, cols], -scale, None, ALU.mult).then_inc(s_("negmax"), 1)
                    if i >= 2:
                        out(i - 2)
                    if i < len(units):
                        dve.wait_ge(s_("exp"), i + 1)
                        cols = slice(sums + nm * i, sums + nm * (i + 1))
                        link(dve.reciprocal(small[:, cols], small[:, cols]))
                        scaled(i).then_inc(s_("probs"), 1)

            units = mla_units()

            def scaled_e(i):
                n = units[i][2]
                return dve.tensor_scalar(pr_e[:, i % 2, 0:n], pr_e[:, i % 2, 0:n], small[:, 32 + i:33 + i], None, ALU.mult)

            def out_e(u):
                h, j, _, _ = units[u]
                cols = slice(j * P, (j + 1) * P)
                dve.wait_ge(sem("mla_ohi"), u + 1)
                dve.tensor_tensor(al[:, HEADS + h, cols], ps[:, 4 + u % 2, 0:P], ah[:, HEADS + h, cols].bitcast(F32),
                                  ALU.subtract).then_inc(sem("mla_out"), 1)

            attention("mla", units, MLA_SCALE, scaled_e, out_e)
            dve.wait_ge(mod_used, P_WIN + 16 + 24)
            take_modulation(1, 0, 48, 6)
            link(scale_pre(1, 0, 8))
            link(scale_post(1, 1, 16))
            link(scale_pre(1, 2, 32))
            scale_post(1, 3, 40).then_inc(scales_ready, 1)

            split(S_WOUT + 5)
            residual(N_EY, lambda k: y_e[:, k, :], 0, 1)
            modulate(N_E2, 1)
            for m in range(NF):
                s = S_GU + m
                split(s + 2)
                dve.wait_ge(sem("silu"), m + 1)
                dve.tensor_tensor(hid[:, m, :], tmp[m % 2], ps[:, 2 * (ordinal(s) % 2) + 1, :], ALU.mult).then_inc(evac_dve, 1)

            def hidden_lo(f):
                dve.wait_ge(sem("hid_hi"), f + 1)
                dve.tensor_tensor(sl[:, f % 2, :], hid[:, f, :], sh[:, f % 2, :].bitcast(F32), ALU.subtract
                                  ).then_inc(sem("hid_lo"), 1)

            hidden_lo(0)
            hidden_lo(1)
            for d in range(NF // 2):
                split(S_DOWN + d + 2)
                if d + 1 < NF // 2:
                    hidden_lo(2 * d + 2)
                    hidden_lo(2 * d + 3)
            dve.wait_ge(w_used, S_DOWN + NF // 2)
            for q in range(2, 4):
                dve.tensor_copy(y2_e[:, 2 * q:2 * q + 2, :], ps[:, 2 * q:2 * q + 2, :]).then_inc(sem("y2_dve"), 1)
            dve.wait_ge(sem("y2_act"), 2)
            residual(N_EF, lambda k: y2_e[:, k, :], 0, 3)
            dve.wait_ge(res_done, 4 * KD)
            dve.memset(small[:, 9:10], 0.0).then_inc(sem("y2_used"), 1)
            modulate(N_O1, 2)

            for p in range(10):
                split(S_OIN + p + 2)
                if 1 <= p <= 6:
                    dve.wait_ge(sem("orope_ps"), p)
                    dst = q_o[:, 2 * p - 2:2 * p, :] if p <= 3 else k_o[:, 2 * p - 8:2 * p - 6, 0:TL]
                    rotate(dst, ps[:, 4 + p % 2, :].rearrange("p (h t) -> p h t", h=2), P, sem("orope_done"), p % 2, 2)
            dve.wait_ge(sem("four_hi"), 1)
            dve.tensor_tensor(al[:, 6:8, 0:TL], ps[:, 2, :].rearrange("p (a b) -> p a b", a=2),
                              ah[:, 6:8, 0:TL].bitcast(F32), ALU.subtract).then_inc(sem("four_lo"), 1)

            ounits = diff_units()

            def scaled_o(i):
                at = 40 + 2 * i
                link(dve.tensor_scalar(small[:, at + 1:at + 2], small[:, at + 1:at + 2], small[:, 7:8], None, ALU.mult))
                link(dve.tensor_scalar(pr_o[:, i % 2, 0, :], pr_o[:, i % 2, 0, :], small[:, at:at + 1], None, ALU.mult))
                return dve.scalar_tensor_tensor(out=pr_o[:, i % 2, 0, :], in0=pr_o[:, i % 2, 1, :],
                                                scalar=small[:, at + 1:at + 2], in1=pr_o[:, i % 2, 0, :],
                                                op0=ALU.mult, op1=ALU.add)

            attention("diff", ounits, DIFF_SCALE, scaled_o, lambda u: None)
            dve.wait_ge(sem("oroot"), 1)
            link(dve.reciprocal(flat(o_rinv[:, :, :]), flat(o_rinv[:, :, :])))
            for h in range(DH + 1):
                if h < DH:
                    dve.scalar_tensor_tensor(out=o_o[:, h, :], in0=o_o[:, h, :], scalar=small[:, 8:9],
                                             in1=o_rinv[:, h, :], op0=ALU.mult, op1=ALU.mult).then_inc(sem("o_ready"), 1)
                if h:
                    dve.wait_ge(sem("o_hi"), h)
                    dve.tensor_tensor(al[:, h - 1, 0:TL], o_o[:, h - 1, :], ah[:, h - 1, 0:TL].bitcast(F32), ALU.subtract
                                      ).then_inc(sem("o_lo"), 1)
            split(S_OOUT + 3)
            residual(N_OY, lambda k: y_o[:, k, :], 1, 1)
            modulate(N_O2, 3, lambda k: h2f[:, k, :])

            def two(at):
                return small[:, at:at + 2]

            def eight(at):
                return small[:, at:at + 16].rearrange("p (t e) -> p t e", t=2)

            L, oh, oh2, t_, gates = eight(16), eight(32), eight(48), eight(64), eight(80)
            v1, v2, idx = two(10), two(12), two(14)
            iota8 = iota[:, 0:NE]
            dve.wait_ge(sem("logits_ps"), 1)
            link(dve.tensor_copy(flat(L), ps[:, 4, 0:16]))

            def pick(values, best, onehot):
                link(dve.tensor_reduce(best, values, AX.X, ALU.max))
                for t in range(2):
                    ins = dve.tensor_scalar(t_[:, t, :], values[:, t, :], best[:, t:t + 1], None, ALU.is_equal)
                link(ins)
                for t in range(2):
                    ins = dve.scalar_tensor_tensor(out=t_[:, t, :], in0=t_[:, t, :], scalar=-float(NE), in1=iota8,
                                                   op0=ALU.mult, op1=ALU.add)
                link(ins)
                link(dve.tensor_reduce(idx, t_, AX.X, ALU.min))
                for t in range(2):
                    ins = dve.tensor_scalar(onehot[:, t, :], t_[:, t, :], idx[:, t:t + 1], None, ALU.is_equal)
                link(ins)

            pick(L, v1, oh)
            link(dve.scalar_tensor_tensor(out=flat(L), in0=flat(oh), scalar=-3.0e38, in1=flat(L), op0=ALU.mult, op1=ALU.add))
            pick(L, v2, oh2)
            dve.tensor_tensor(small[:, 2:4], v2, v1, ALU.subtract).then_inc(sem("top_diff"), 1)
            dve.wait_ge(sem("top_exp"), 1)
            link(dve.tensor_scalar(v1, small[:, 4:6], 1.0, None, ALU.add))
            link(dve.reciprocal(v1, v1))
            link(dve.tensor_tensor(v2, small[:, 4:6], v1, ALU.mult))
            for t in range(2):
                ins = dve.tensor_scalar(gates[:, t, :], oh[:, t, :], v1[:, t:t + 1], None, ALU.mult)
            link(ins)
            for t in range(2):
                ins = dve.scalar_tensor_tensor(out=gates[:, t, :], in0=oh2[:, t, :], scalar=v2[:, t:t + 1],
                                               in1=gates[:, t, :], op0=ALU.mult, op1=ALU.add)
            link(ins)
            dve.tensor_tensor(flat(oh), flat(oh), flat(oh2), ALU.add).then_inc(sem("mask_ready"), 1)
            link(dve.memset(flat(rg[:, :, :]), -1.0))
            for t in range(2):
                ins = dve.tensor_copy(rg[:, 0:NE, 2 + t], gates[:, t, :])
            dve.wait_ge(sem("rank_ps"), 1)
            link(dve.scalar_tensor_tensor(out=flat(t_), in0=ps[:, 4, 16:32], scalar=1.0, in1=flat(oh), op0=ALU.add, op1=ALU.mult))
            for t in range(2):
                ins = dve.tensor_scalar(rg[:, 0:NE, t], t_[:, t, :], -1.0, None, ALU.add)
            link(ins)
            dve.tensor_reduce(cnt[:, :], ps[:, 4, 32:40], AX.X, ALU.max).then_inc(sem("count_ready"), 1)
            for t in range(2):
                dve.wait_ge(sem("tok_hi"), t + 1)
                dve.tensor_tensor(h2l[:, t, :], ps[:, 2 * t:2 * t + 2, :].rearrange("p a b -> p (a b)"),
                                  h2h[:, t, :].bitcast(F32), ALU.subtract).then_inc(sem("tok_lo"), 1)
            dve.memset(acc, 0.0).then_inc(sem("acc_done"), 1)

            def select(e):
                link_in_loop(dve.tensor_copy(cur, rg[:, bass.ds(e, 1), :].rearrange("p o c -> p (o c)")))
                for t in range(2):
                    ins = dve.tensor_scalar(sel[:, t, :], iota, cur[:, t:t + 1], None, ALU.is_equal)
                ins.then_inc(sem("sel_ready"), 1)

            cur_count = [None]

            def link_in_loop(ins):
                ins.then_inc(sem("cur_ready"), 1)
                dve.wait_ge(sem("cur_ready"), cur_count[0])

            def gathered(idx):
                dve.wait_ge(sem("xl_ps"), idx)
                dve.tensor_copy(flat(xel[:, :, :]), ps[:, 0:2, :].rearrange("p a b -> p (a b)")).then_inc(sem("xe_l"), 1)

            def experts(ps_no):
                base, gb, ab = S_MOE + MOE_PIECES * ps_no, 88 * ps_no, 9 * ps_no

                def split_q(e, q):
                    dve.wait_ge(w_hi, PER_EXPERT * e + (base + q + 1))
                    dve.tensor_tensor(wl[:, q % SPLITS, :], slot(q % SLOTS), wh[:, q % SPLITS, :].bitcast(F32),
                                      ALU.subtract).then_inc(w_lo, 1)

                cur_count[0] = ab + 1
                select(0)
                if ps_no == 0:
                    for q in range(AHEAD):
                        split_q(0, q)
                gathered(ab + 1)
                with dve.Fori(0, NE) as e:
                    for q, (kind, g, half) in enumerate(ORDER):
                        if kind == "gu" and half == 1:
                            dve.wait_ge(sem("moe_silu"), 11 * e + (gb + g + 1))
                            gu = ps[:, g % 2, :].rearrange("p (b w c) -> p b w c", b=2, w=2)
                            dve.tensor_tensor(hh(g).rearrange("p (b c) -> p b c", b=2),
                                              silu_t(g).rearrange("p (b c) -> p b c", b=2), gu[:, :, 1, :],
                                              ALU.mult).then_inc(sem("moe_hid"), 1)
                        if q == 32:
                            dve.wait_ge(sem("y_h"), e + (8 * ps_no + 1))
                            dve.scalar_tensor_tensor(out=yl, in0=ps[:, 2:4, :].rearrange("p a b -> p (a b)"),
                                                     scalar=gslot, in1=yh.bitcast(F32), op0=ALU.mult,
                                                     op1=ALU.subtract).then_inc(sem("y_l"), 1)
                        split_q(e, q + AHEAD)
                        turned = {3: 0, 4: 1}.get(q, g + 1 if kind == "d" and 1 <= g <= 9 else None)
                        if turned is not None:
                            dve.wait_ge(sem("hT_hi"), 11 * e + (gb + turned + 1))
                            dve.tensor_tensor(sl[:, turned % 2, 0:256], ps[:, 4, 0:256],
                                              sh[:, turned % 2, 0:256].bitcast(F32), ALU.subtract).then_inc(sem("hT_lo"), 1)
                        if q == 28:
                            dve.wait_ge(sem("selT_ps"), e + (8 * ps_no + 1))
                            cur_count[0] = e + (ab + 2)
                            select(e + 1)
                        if q == 31:
                            gathered(e + (ab + 2))
                    for c in range(4):
                        dve.wait_ge(sem("scat_ps"), 4 * e + (32 * ps_no + c + 1))
                        dve.tensor_tensor(acc[:, 2 * c:2 * c + 2, :], acc[:, 2 * c:2 * c + 2, :],
                                          ps[:, 5 + c % 2, :].rearrange("p (a b) -> p a b", a=2), ALU.add
                                          ).then_inc(sem("acc_done"), 1)

            experts(0)
            dve.wait_ge(sem("count_ready"), 1)
            most = dve.value_load(cnt[0:1, 0:1], min_val=0, max_val=TL)
            with dve.If(most > P):
                dve.tensor_scalar(rg[:, :, 0:2], rg[:, :, 0:2], -float(P), None, ALU.add).then_inc(sem("ranks_moved"), 1)
                dve.wait_ge(sem("ranks_moved"), 1)
                experts(1)
            dve.memset(small[:, 0:1], 0.0).then_inc(sem("acc_final"), 1)
            residual(N_OF, lambda k: acc[:, k, :], 1, 3)

        @block.tensor
        def _(pe):
            def mm3(out, lh, ll, rh, rl, start, stop):
                pe.matmul(out, lh, rh, start=start, stop=False)
                pe.matmul(out, lh, rl, start=False, stop=False)
                return pe.matmul(out, ll, rh, start=False, stop=stop)

            def sum_squares(n):
                K, W = NORMS[n]
                if n:
                    pe.wait_ge(root_ready, n)
                for k in range(K):
                    j = chunks_before(n) + k
                    pe.wait_ge(sq_ready, j + 1)
                    pe.matmul(ps[:, 4, 0:W], ones, sq[:, j % 2, 0:W], start=(k == 0), stop=(k == K - 1)
                              ).then_inc(ssq_done, 1)

            def modulation(i, bank, m0):
                n = slot_of(i)
                pe.wait_ge(landed[n], 16 * landings(i))
                for c in range(2):
                    for k in range(KD):
                        mm = pe.matmul(ps[:, bank, 2 * (m0 + c):2 * (m0 + c) + 2],
                                       slot(n)[:, k * 256 + c * P:k * 256 + (c + 1) * P], condS[:, k, :],
                                       start=(k == 0), stop=(k == KD - 1))
                mm.then_inc(mod_used, 1)

            def piece(s, W, first=None, widths=(P, P), tokens=False):
                pe.wait_ge(w_lo, s + 1)
                c0 = ordinal(s)
                if c0 >= 2:
                    last = s - 2 if s not in (S_OIN, S_OIN + 1) else s - 2 - (S_OIN - S_DOWN)
                    if evacs(last, "act"):
                        pe.wait_ge(evac_act, evacs(last, "act"))
                    if evacs(last, "dve"):
                        pe.wait_ge(evac_dve, evacs(last, "dve"))
                bank = 2 * (c0 % 2)
                b = s % SPLITS
                if tokens:
                    for t in range(4):
                        for k in range(KD):
                            mm = mm3(ps[:, bank + t // 2, (t % 2) * 256:(t % 2) * 256 + 256],
                                     ah[:, k, t * P:(t + 1) * P], al[:, k, t * P:(t + 1) * P],
                                     wh[:, b, k * 256:(k + 1) * 256], wl[:, b, k * 256:(k + 1) * 256],
                                     k == 0, k == KD - 1)
                else:
                    for c in range(2):
                        for k in range(KD):
                            if first and c == 0:
                                first(k)
                            at = k * 256 + c * P
                            mm = mm3(ps[:, bank + c, 0:W], wh[:, b, at:at + P], wl[:, b, at:at + P],
                                     ah[:, k, 0:W], al[:, k, 0:W], k == 0, k == KD - 1)
                mm.then_inc(w_used, 1)

            pe.wait_ge(sem("cst_loaded"), 16)
            sum_squares(N_E1)
            pe.wait_ge(sem("lam_prod"), 1)
            pe.matmul(ps[:, 5, 0:2], ones[0:64, :], small[0:64, 0:2], start=True, stop=True).then_inc(sem("lam_sums"), 1)
            pe.wait_ge(cond_ready, 1)
            for i in range(P_MOD_A, P_WIN):
                modulation(i, 7, 2 * i)
            for p in range(9):
                piece(S_WIN + p, T, (lambda k: pe.wait_ge(mod_lo, k + 1)) if p == 0 else None)
            sum_squares(N_Q)
            sum_squares(N_KV)
            for i in range(16):
                modulation(P_MOD_B + i, 7, 16 + 2 * i)

            jobs = []
            for h in range(HEADS):
                jobs.append((P, [(uq[:, k, h * 192:h * 192 + P], zq[:, k, :]) for k in range(QR)]))
            for h in range(HEADS):
                jobs.append((64, [(uq[:, k, h * 192 + P:h * 192 + 192], zq[:, k, :]) for k in range(QR)]))
            for h in range(HEADS):
                jobs.append((P, [(ukv[:, k, h * 256:h * 256 + P], zkv[:, k, :]) for k in range(KVR)]))
            for t in range(4):
                jobs.append((P, [(zkv[:, k, t * P:(t + 1) * P],
                                  ukv[:, k, :].rearrange("p (h c) -> p h c", h=HEADS)[:, :, P:256]) for k in range(KVR)]))
            pe.wait_ge(sem("uq_loaded"), 16)
            pe.wait_ge(sem("ukv_loaded"), 16)
            pe.wait_ge(t_ready, chunks_before(N_KV))
            pe.wait_ge(evac_act, evacs(S_WIN + 8, "act"))
            pe.wait_ge(evac_dve, evacs(S_WIN + 8, "dve"))
            pe.matmul(ps[0:64, 5, 0:TL], rot[0:64, 0:64], k_pe[0:64, 0:TL], start=True, stop=True).then_inc(sem("rope_ps"), 1)
            pe.wait_ge(sem("conv_lo"), HEADS)
            for n, (w, parts) in enumerate(jobs):
                if n >= 4:
                    pe.wait_ge(sem("proj_ready"), n - 3)
                if n == 2 * HEADS:
                    pe.wait_ge(t_ready, chunks_before(N_KV) + KVR)
                for k, (l, r) in enumerate(parts):
                    mm = pe.matmul(ps[0:w, n % 4, :], l, r, start=(k == 0), stop=(k == len(parts) - 1))
                mm.then_inc(sem("proj_ps"), 1)
                if n == 11:
                    pe.wait_ge(scales_ready, 2)
                    for g in range(2):
                        pe.matmul(ps[0:64, 6 + g, :], rot[0:64, 0:64], q_pe[0:64, 2 * g:2 * g + 2, 0:TL],
                                  start=True, stop=True).then_inc(sem("rope_ps"), 1)

            def attention(name, units, scores, pv, pr, filler):
                s_ = lambda k: sem(f"{name}_{k}")
                tb, ob = (2, 4) if name == "mla" else (4, 6)
                pt = pt_e if name == "mla" else pt_o
                for i in range(len(units) + 2):
                    if i < len(units):
                        if i >= 2:
                            pe.wait_ge(s_("exp"), i - 1)
                        scores(i).then_inc(s_("scores"), 1)
                    filler(i)
                    if 1 <= i <= len(units):
                        u = i - 1
                        pe.wait_ge(s_("probs"), u + 1)
                        if u >= 2:
                            pe.wait_ge(s_("pt"), u - 1)
                        for b in range(units[u][2] // P):
                            mm = pe.transpose(ps[:, tb + u % 2, b * P:(b + 1) * P], pr(u, b), ident)
                        mm.then_inc(s_("turned"), 1)
                    if i >= 2:
                        u = i - 2
                        pe.wait_ge(s_("pt"), u + 1)
                        if u >= 2:
                            pe.wait_ge(s_("out"), u - 1)
                        nb = units[u][2] // P
                        for b in range(nb):
                            mm = pe.matmul(ps[:, ob + u % 2, 0:P], pv(u, b), pt[:, u % 2, b * P:(b + 1) * P],
                                           start=(b == 0), stop=(b == nb - 1))
                        mm.then_inc(s_("pv"), 1)

            units = mla_units()
            pe.wait_ge(sem("proj_ready"), len(jobs))
            pe.wait_ge(sem("rope_done"), 3)

            def scores_e(i):
                h, j, n, k0 = units[i]
                pe.matmul(ps[:, i % 2, 0:n], q_nope[:, h, j * P:(j + 1) * P], k_nope[:, h, k0:k0 + n], start=True, stop=False)
                return pe.matmul(ps[:, i % 2, 0:n], q_pe[0:64, h, j * P:(j + 1) * P], k_pe[0:64, k0:k0 + n],
                                 start=False, stop=True)

            def filler_e(i):
                first, last = (24 * i) // (len(units) + 2), (24 * (i + 1)) // (len(units) + 2)
                for n in range(first, last):
                    modulation(P_MOD_O + n, 6, 2 * n)

            attention("mla", units, scores_e,
                      lambda u, b: v_e[:, units[u][3] // P + b, units[u][0] * P:(units[u][0] + 1) * P],
                      lambda u, b: pr_e[:, u % 2, b * P:(b + 1) * P], filler_e)
            pe.wait_ge(sem("mla_out"), len(units))
            pe.wait_ge(sem("mla_pt"), len(units))
            for p in range(4):
                piece(S_WOUT + p, T)
            sum_squares(N_EY)
            sum_squares(N_E2)
            for m in range(NF):
                piece(S_GU + m, T, (lambda k: pe.wait_ge(mod_lo, KD + k + 1)) if m == 0 else None)

            pe.wait_ge(evac_dve, evacs(S_GU + NF - 1, "dve"))
            for f in range(NF):
                s = S_DOWN + f // 2
                if f % 2 == 0:
                    pe.wait_ge(w_lo, s + 1)
                pe.wait_ge(sem("hid_lo"), f + 1)
                for m in range(KD):
                    at = (f % 2) * D + m * P
                    mm = mm3(ps[:, m, :], wh[:, s % SPLITS, at:at + P], wl[:, s % SPLITS, at:at + P],
                             sh[:, f % 2, :], sl[:, f % 2, :], f == 0, f == NF - 1)
                mm.then_inc(w_used if f % 2 else sem("f_used"), 1)
            pe.wait_ge(sem("y2_act"), 2)
            pe.wait_ge(sem("y2_dve"), 2)
            sum_squares(N_EF)
            sum_squares(N_O1)

            def turn(p):
                src = q_o[:, 2 * p:2 * p + 2, :] if p < 3 else k_o[:, 2 * p - 6:2 * p - 4, 0:TL]
                pe.wait_ge(evac_act, evacs(S_OIN + p, "act"))
                if p >= 2:
                    pe.wait_ge(sem("orope_done"), p - 1)
                else:
                    pe.wait_ge(root_ready, N_O1 + 1)
                pe.matmul(ps[:, 4 + (p + 1) % 2, :], rot, src, start=True, stop=True).then_inc(sem("orope_ps"), 1)

            for p in range(10):
                W = T if 3 <= p < 6 else TL
                piece(S_OIN + p, W, (lambda k: pe.wait_ge(mod_lo, 2 * KD + k + 1)) if p == 0 else None, tokens=(6 <= p < 9))
                if 1 <= p <= 6:
                    turn(p - 1)
            pe.wait_ge(sem("dftc_loaded"), 16)
            pe.wait_ge(sem("dftt_loaded"), 16)
            pe.wait_ge(evac_act, evacs(S_OIN + 9, "act"))
            for t in range(2):
                for c in range(2):
                    mm = pe.matmul(ps[:, t, c * 256:(c + 1) * 256], f_o[:, c, t * P:(t + 1) * P], dftc, start=True, stop=True)
            mm.then_inc(sem("four_ps"), 1)
            pe.wait_ge(sem("four_mid"), 1)
            for c in range(2):
                for n in range(4):
                    t, part = n // 2, n % 2
                    mm = pe.matmul(ps[:, 2, c * TL:(c + 1) * TL], mid[:, 2 * t + c, part * P:(part + 1) * P],
                                   dftt[:, 2 * t + part, :], start=(n == 0), stop=(n == 3))
            mm.then_inc(sem("four_ps"), 1)

            ounits = diff_units()
            pe.wait_ge(sem("four_lo"), 1)
            pe.wait_ge(sem("orope_done"), 6)

            def scores_o(i):
                h, j, n, _ = ounits[i]
                for m in range(2):
                    mm = pe.matmul(ps[:, 2 * (i % 2) + m, :], q_o[64 * m:64 * m + 64, h, j * P:(j + 1) * P],
                                   k_o[64 * m:64 * m + 64, h, :], start=True, stop=True)
                return mm

            attention("diff", ounits, scores_o, lambda u, b: v_o[:, b, ounits[u][0] * P:(ounits[u][0] + 1) * P],
                      lambda u, b: pr_o[:, u % 2, 0, b * P:(b + 1) * P], lambda i: None)
            pe.wait_ge(sem("osq_ready"), 1)
            for n in range(3):
                pe.matmul(ps[:, n, :], ones, o_sq[:, 2 * n:2 * n + 2, :], start=True, stop=True).then_inc(sem("ossq_done"), 1)
            pe.wait_ge(sem("o_lo"), DH)
            for p in range(4):
                piece(S_OOUT + p, TL)
            sum_squares(N_OY)
            sum_squares(N_O2)

            pe.wait_ge(mod_h, 3 * 2 * KD + KD)
            pe.wait_ge(root_ready, N_O2 + 1)
            router = vc("router").rearrange("p (k e) -> p k e", k=KD)
            for t in range(2):
                for k in range(KD):
                    mm = pe.matmul(ps[:, 4, 8 * t:8 * t + 8], h2f[:, k, t * P:(t + 1) * P], router[:, k, :],
                                   start=(k == 0), stop=(k == KD - 1))
            mm.then_inc(sem("logits_ps"), 1)
            for t in range(2):
                for k in range(KD):
                    mm = pe.transpose(ps[:, 2 * t + k // 4, (k % 4) * P:(k % 4 + 1) * P], h2f[:, k, t * P:(t + 1) * P], ident)
                mm.then_inc(sem("tok_ps"), 1)
            pe.wait_ge(sem("mask_ready"), 1)
            mask = [small[:, 32 + 8 * t:40 + 8 * t] for t in range(2)]
            pe.matmul(ps[:, 4, 16:24], tri, mask[0], start=True, stop=True)
            pe.matmul(ps[:, 4, 24:32], ones, mask[0], start=True, stop=False)
            pe.matmul(ps[:, 4, 24:32], tri, mask[1], start=False, stop=True)
            pe.matmul(ps[:, 4, 32:40], ones, mask[0], start=True, stop=False)
            pe.matmul(ps[:, 4, 32:40], ones, mask[1], start=False, stop=True).then_inc(sem("rank_ps"), 1)
            pe.wait_ge(sem("tok_lo"), 2)
            pe.wait_ge(sem("count_ready"), 1)

            def gather(idx, added):
                pe.wait_ge(sem("sel_ready"), idx)
                pe.wait_ge(sem("acc_done"), added)
                for src, bank, done in ((h2h, 5, "xh_ps"), (h2l, 0, "xl_ps")):
                    for k in range(KD):
                        for t in range(2):
                            mm = pe.matmul(ps[:, bank + k // 4, (k % 4) * P:(k % 4 + 1) * P],
                                           src[:, t, k * P:(k + 1) * P], sel[:, t, :], start=(t == 0), stop=(t == 1))
                    mm.then_inc(sem(done), 1)

            def experts(ps_no):
                base, gb, ab = S_MOE + MOE_PIECES * ps_no, 88 * ps_no, 9 * ps_no

                def turn_hidden(e, g):
                    pe.wait_ge(sem("moe_hid"), 11 * e + (gb + g + 1))
                    for b in range(2):
                        mm = pe.transpose(ps[:, 4, b * P:(b + 1) * P], hh(g)[:, b * P:(b + 1) * P], ident)
                    mm.then_inc(sem("hid_T"), 1)

                gather(ab + 1, 32 * ps_no + 1)
                with pe.Fori(0, NE) as e:
                    for q, (kind, g, half) in enumerate(ORDER):
                        b = q % SPLITS
                        if q == 0:
                            pe.wait_ge(sem("xe_h"), e + (ab + 1))
                            pe.wait_ge(sem("xe_l"), e + (ab + 1))
                        if q == 32:
                            gather(e + (ab + 2), 4 * e + (32 * ps_no + 1))
                        pe.wait_ge(w_lo, PER_EXPERT * e + (base + q + 1))
                        if kind == "gu":
                            for k in range(4):
                                kk = 4 * half + k
                                mm = mm3(ps[:, g % 2, :], xeh[:, kk, :], xel[:, kk, :], wh[:, b, k * 512:(k + 1) * 512],
                                         wl[:, b, k * 512:(k + 1) * 512], kk == 0, kk == KD - 1)
                        else:
                            pe.wait_ge(sem("hT_lo"), 11 * e + (gb + g + 1))
                            for f in range(2):
                                for c in range(2):
                                    at = f * D + c * 512
                                    mm = mm3(ps[:, 2 + c, :], sh[:, g % 2, f * P:(f + 1) * P], sl[:, g % 2, f * P:(f + 1) * P],
                                             wh[:, b, at:at + 512], wl[:, b, at:at + 512],
                                             g == 0 and f == 0, g == 10 and f == 1)
                        mm.then_inc(w_used, 1)
                        if q == 3:
                            turn_hidden(e, 0)
                            for t in range(2):
                                pe.transpose(ps[:, 7, t * P:(t + 1) * P], sel[:, t, :].bitcast(F32), ident)
                            pe.matmul(ps[:, 7, TL:TL + 1], sel[:, 0, :].bitcast(F32), cur[:, 2:3], start=True, stop=False)
                            pe.matmul(ps[:, 7, TL:TL + 1], sel[:, 1, :].bitcast(F32), cur[:, 3:4], start=False, stop=True
                                      ).then_inc(sem("selT_ps"), 1)
                        if kind == "d" and g <= 9:
                            turn_hidden(e, g + 1)
                    pe.wait_ge(sem("selT_ready"), e + (8 * ps_no + 1))
                    pe.wait_ge(sem("y_l"), e + (8 * ps_no + 1))
                    pe.wait_ge(sem("xe_h"), e + (ab + 2))
                    for c in range(4):
                        if c >= 2:
                            pe.wait_ge(sem("acc_done"), 4 * e + (32 * ps_no + c))
                        for k in (2 * c, 2 * c + 1):
                            out = ps[:, 5 + c % 2, (k % 2) * TL:(k % 2 + 1) * TL]
                            pe.matmul(out, yh[:, k * P:(k + 1) * P], selT, start=True, stop=False)
                            mm = pe.matmul(out, yl[:, k * P:(k + 1) * P], selT, start=False, stop=True)
                        mm.then_inc(sem("scat_ps"), 1)

            experts(0)
            most = pe.value_load(cnt[0:1, 0:1], min_val=0, max_val=TL)
            with pe.If(most > P):
                experts(1)
            sum_squares(N_OF)


def mla_units():
    return [(h, j, T if j < 2 else TL, 0 if j < 2 else TL) for h in range(HEADS) for j in range(4)]


def diff_units():
    return [(h, j, T, 0) for h in range(DH) for j in range(2)]


def _chunked(w):
    return w.reshape(-1, P, w.shape[-1]).transpose(1, 0, 2)


def _columns(w):
    n = w.shape[1] // 256
    return w.reshape(KD, P, n, 256).transpose(2, 1, 0, 3).reshape(n, P, PIECE)


def _rows(w):
    n = w.shape[0] // 256
    return w.reshape(n, 2, P, D).transpose(0, 2, 1, 3).reshape(n, P, PIECE)


def _constants():
    cst = np.zeros((P, 5, P), np.float32)
    r = np.arange(P)
    cst[r, 0, r] = 1.0
    cst[:, 1, :] = 1.0
    cst[:, 2, :] = r[:, None] < r[None, :]
    cst[:, 3, :] = r[None, :]
    for m in range(P):
        if m % 64 < 32:
            cst[m + 32, 4, m] = -1.0
        else:
            cst[m - 32, 4, m] = 1.0
    t = np.arange(TL)
    inv = (np.float32(10000.0) ** (-np.arange(16, dtype=np.float32) / np.float32(16))).astype(np.float32)
    row, col = (t // 64).astype(np.float32), (t % 64).astype(np.float32)
    ang = np.concatenate([row[:, None] * inv, col[:, None] * inv], -1)
    ang = ang.T[r % 32]
    rope = np.stack([np.cos(ang), np.sin(ang)], 1).astype(np.float32)
    c = np.arange(64)
    a = 2 * np.pi * ((c[:, None] * c[None, :]) % 64) / 64
    dft = np.zeros((P, 1280), np.float32)
    for g in range(2):
        dft[g * 64:(g + 1) * 64, g * 64:(g + 1) * 64] = np.cos(a)
        dft[g * 64:(g + 1) * 64, P + g * 64:P + (g + 1) * 64] = np.sin(a)
    a = 2 * np.pi * ((t[:, None] * t[None, :]) % TL) / TL
    norm = math.sqrt(TL * 64)
    both = np.stack([np.cos(a), -np.sin(a)]) / norm
    dft[:, 256:] = both.reshape(2, 2, P, TL).transpose(2, 1, 0, 3).reshape(P, 1024)
    return cst, rope, dft


def kernel(x, c, ctx, c_ctx, ev_mod_w, ev_mod_b, ev_norm_g, ev_w_in, ev_conv_w, ev_q_norm_g, ev_w_uq,
           ev_kv_norm_g, ev_w_ukv, ev_w_out, ev_ffn_gate, ev_ffn_up, ev_ffn_down, od_mod_w, od_mod_b,
           od_norm_g, od_w_in, od_lambda, od_subln_g, od_w_out, od_router, od_exp_gate, od_exp_up, od_exp_down):
    import concourse.bacc as _bacc
    from concourse.bass_utils import run_bass_kernel_spmd as _run

    A = np.asarray
    xT = _chunked(np.concatenate([A(x)[0], A(ctx)[0]], 0).T)
    per_part = lambda v: A(v).reshape(-1, P).T
    twice = lambda v: np.repeat(per_part(v)[:, :, None], 2, 2).reshape(P, -1)
    lam = np.zeros((P, 4), np.float32)
    lam[0:64] = A(od_lambda)[0].T
    vec = np.concatenate([
        np.stack([per_part(A(c)[0]), per_part(A(c_ctx))], 2).reshape(P, 16),
        twice(A(ev_mod_b)[0]), twice(A(od_mod_b)[0]), twice(A(ev_norm_g)[0]), twice(A(od_norm_g)[0]),
        A(ev_conv_w)[0].reshape(3, 4, P).transpose(2, 0, 1).reshape(P, 12),
        per_part(A(ev_q_norm_g)[0]), per_part(A(ev_kv_norm_g)[0]), per_part(A(od_subln_g)[0]), lam,
        _chunked(A(od_router)[0]).reshape(P, 64)], 1)
    cst, rope, dft = _constants()

    stream = np.empty((P_MOE + MOE_PIECES + AHEAD, P, PIECE), np.float32)
    mod = _columns(A(ev_mod_w)[0])
    stream[P_MOD_A:P_WIN] = mod[:8]
    stream[P_MOD_B:P_MOD_O] = mod[8:]
    w = A(ev_w_in)[0]
    order = [w[:, 0:512]]
    for j in range(4):
        order += [w[:, 512 + j * P:640 + j * P], w[:, 1024 + j * P:1152 + j * P]]
    order += [w[:, 1536:], np.zeros((D, 64), np.float32)]
    stream[P_WIN:P_MOD_B] = _columns(np.concatenate(order, 1))
    stream[P_MOD_O:P_WOUT] = _columns(A(od_mod_w)[0])
    at = P_WOUT
    g, u = (A(v)[0].reshape(D, NF, 1, P) for v in (ev_ffn_gate, ev_ffn_up))
    for part in (_columns(A(ev_w_out)[0]), _columns(np.concatenate([g, u], 2).reshape(D, 2 * FF)), _rows(A(ev_ffn_down)[0]),
                 _columns(A(od_w_in)[0]), _columns(A(od_w_out)[0])):
        stream[at:at + len(part)] = part
        at += len(part)
    gate, up, down = A(od_exp_gate)[0], A(od_exp_up)[0], A(od_exp_down)[0]
    gu_at = [q for q, o in enumerate(ORDER) if o[0] == "gu"]
    d_at = [q for q, o in enumerate(ORDER) if o[0] == "d"]
    for e in range(NE):
        own = stream[P_MOE + e * PER_EXPERT:P_MOE + (e + 1) * PER_EXPERT]
        both = np.stack([gate[e].reshape(D, NF, P), up[e].reshape(D, NF, P)], 2)
        both = both.reshape(2, 4, P, 11, 512).transpose(3, 0, 2, 1, 4)
        own[gu_at] = both.reshape(22, P, PIECE)
        own[d_at] = _rows(down[e])
    stream[P_MOE + MOE_PIECES:] = stream[P_MOE:P_MOE + AHEAD]

    arrays = {"x": xT, "vec": vec, "cst": cst, "rope": rope, "dft": dft, "uq": _chunked(A(ev_w_uq)[0]),
              "ukv": _chunked(A(ev_w_ukv)[0]), "w": stream}
    arrays = {f"in_{n}": np.ascontiguousarray(v) for n, v in arrays.items()}
    nc = _bacc.Bacc("TRN2", target_bir_lowering=False, num_devices=1)
    aps = [nc.dram_tensor(n, v.shape, mybir.dt.from_np(v.dtype), kind="ExternalInput").ap() for n, v in arrays.items()]
    out = nc.dram_tensor("out", (P, KD, TL), F32, kind="ExternalOutput").ap()
    build(nc, *aps, out)
    r = _run(nc, [arrays], core_ids=[0])
    return r.results[0]["out"].transpose(2, 1, 0).reshape(1, TL, D)
```

```python
import math
from contextlib import ExitStack

import concourse.bass as bass
import numpy as np
from concourse import mybir

ALU = mybir.AluOpType
ACT = mybir.ActivationFunctionType
AX = mybir.AxisListType
F32 = mybir.dt.float32
F32R = mybir.dt.float32r
I32 = mybir.dt.int32

P = 128
D = 1024
KD = D // P
TL = 256
T = 512
FF = 2816
NF = FF // P
NE = 8
EPS = 1e-6
HEADS = 4
QR, KVR = 3, 2
MLA_SCALE = (128 + 64) ** -0.5
DH = 6
DIFF_SCALE = 64 ** -0.5
LAM_INIT = 0.8 - 0.6 * math.exp(-0.3)

PIECE = 2048
N_MOD = 48
MOD_FIRST, MOD_WIN = 8, 18
WIN = 9
S_WOUT, S_GU, S_DOWN, S_OIN, S_OOUT, S_MOE = 57, 61, 83, 94, 104, 108
PER_EXPERT = 33
MOD_GAP = 6
AHEAD = 3
MOE_STREAM = 2 + NE * PER_EXPERT + AHEAD
EARLY_SLOTS = 3
SLOTS = 11
SPLITS = 3


def s_win(p):
    return MOD_FIRST + 3 * p


def s_mod(n):
    if n < MOD_FIRST:
        return n
    m = n - MOD_FIRST
    return MOD_FIRST + 3 * (m // 2) + 1 + m % 2 if m < MOD_WIN else MOD_FIRST + WIN + MOD_WIN + m - MOD_WIN


VEC = {}
_at = 0
for _n, _w in (("cond", 16), ("mod_b0", 96), ("mod_b1", 96), ("norm0", 64), ("norm1", 64), ("conv", 12),
               ("qn", QR), ("kvn", KVR), ("subln", 1), ("lam", 4), ("router", 64)):
    VEC[_n] = (_at, _w)
    _at += _w
NVEC = _at

NORMS = [(KD, T), (QR, T), (KVR, T), (KD, T), (KD, T), (KD, T), (KD, T), (KD, TL), (KD, TL), (KD, TL)]
N_E1, N_Q, N_KV, N_EY, N_E2, N_EF, N_O1, N_OY, N_O2, N_OF = range(10)
NDIM = [D, QR * P, KVR * P] + [D] * 7


def chunks_before(n):
    return sum(k for k, _ in NORMS[:n])


RES_BEFORE = {N_E1: 0, N_EY: 0, N_E2: 2 * KD, N_EF: 2 * KD, N_O1: 4 * KD, N_OY: 4 * KD, N_O2: 5 * KD, N_OF: 5 * KD}


def expert_order():
    order = []
    for g in range(1, 10):
        order += [("gu", g, 0), ("gu", g, 1), ("d", g - 1, 0)]
    order[-1:] = [("gu", 10, 0), ("gu", 10, 1), ("d", 8, 0), ("d", 9, 0)]
    return order + [("gu", 0, 0), ("gu", 0, 1), ("d", 10, 0)]


ORDER = expert_order()
HEAD_SUMS = (0, 1, 5)
GATHER = ORDER.index(("gu", 10, 1))
TURN = {q: (g + 1) % 11 for q, (kind, g, _) in enumerate(ORDER) if kind == "d" and g != 8}
TURN[GATHER] = 9
SCATTER = (0, 2, 6, 7)


def build(nc, x_d, vec_d, cst_d, rope_d, dft_d, uq_d, ukv_d, w_d, out_d):
    with ExitStack() as ctx:
        def sb(name, shape, dt=F32):
            return ctx.enter_context(nc.sbuf_tensor(name, shape, dt))

        sems = {}

        def sem(name):
            if name not in sems:
                sems[name] = ctx.enter_context(nc.semaphore(name))
            return sems[name]

        ps = ctx.enter_context(nc.psum_tensor("ps", [P, 8, 512], F32))
        raw = sb("raw", [P, SLOTS * PIECE])
        wh = sb("wh", [P, SPLITS, PIECE], F32R)
        wl = sb("wl", [P, SPLITS, PIECE], F32R)
        ah = sb("ah", [P, KD, T], F32R)
        al = sb("al", [P, KD, T], F32R)
        sh = sb("sh", [P, 2, T], F32R)
        sl = sb("sl", [P, 2, T], F32R)
        x = sb("x", [P, KD, T])
        cst = sb("cst", [P, 5, P])
        ident, ones, tri, iota, rot = (cst[:, i, :] for i in range(5))
        rope = sb("rope", [P, 2, TL])
        vec = sb("vec", [P, NVEC])
        condS = vec[:, VEC["cond"][0]:VEC["cond"][0] + 16].rearrange("p (k c) -> p k c", k=KD)
        mod0 = sb("mod0", [P, 48, 2])
        mod1 = sb("mod1", [P, 48, 2])
        scl = sb("scl", [P, 2, 4, KD, 2])
        eps = sb("eps", [P, 1])
        rinv = sb("rinv", [P, T])
        sq = sb("sq", [P, 2, T])
        t2 = sb("t2", [P, T])
        small = sb("small", [P, 96])
        cnt = sb("cnt", [P, 1], I32)
        rg = rope[:, 0, 0:4 * (NE + 1)].rearrange("p (e c) -> p e c", c=4)
        cur = rope[:, 1, 0:4]
        sel = sh[:, 1, 256:512].rearrange("p (t s) -> p t s", t=2)
        selT = sh[:, 0, 256:512]
        gslot = rope[:, 1, 8:9]

        H0 = EARLY_SLOTS * PIECE

        def area(at, *dims):
            n = int(np.prod(dims))
            v = raw[:, H0 + at:H0 + at + n]
            if len(dims) == 2:
                v = v.rearrange("p (a b) -> p a b", a=dims[0])
            if len(dims) == 3:
                v = v.rearrange("p (a b c) -> p a b c", a=dims[0], b=dims[1])
            return v

        t3 = area(15872, T)
        tmp = [t2[:, :], t3]
        b_gate = area(0, HEADS, T)
        q_nope = area(0, HEADS, T)
        q_pe = area(2048, HEADS, T)
        cu = area(4096, HEADS * 2, 258).rearrange("p (c s) t -> p c s t", s=2)
        k_nope = area(4096, HEADS, T)
        v_e = area(6160, 4, T)
        uq = area(8208, QR, 768)
        ukv = area(10512, KVR, 1024)
        zq = area(12560, QR, T)
        zkv = area(14096, KVR, T)
        k_pe = area(15120, T)
        pr_e = area(12560, 2, T)
        pt_e = area(13584, 2, T)
        xn = area(8208, KD, T)
        mod_row = area(2048, 2, 256)
        y_e = area(0, KD, T)
        hid = area(0, NF, T)
        y2_e = area(11264, KD, T)
        q_o = area(0, DH, TL)
        k_o = area(1536, DH, T)
        v_o = area(4608, 4, 768)
        f_o = area(7680, 2, TL)
        mid = area(8192, 4, 256)
        dftc = area(9216, 256)
        dftt = area(9472, 4, 256)
        o_o = area(10496, DH, TL)
        pr_o = area(12032, 2, 2, T)
        pt_o = area(14080, 2, T)
        o_sq = area(7680, DH, TL)
        o_rinv = o_sq
        y_o = area(0, KD, TL)
        h2f = x[:, :, TL:T]
        h2h, h2l = (a[:, 0:4, :].rearrange("p a b -> p (a b)").rearrange("p (t f) -> p t f", t=2) for a in (ah, al))
        xeh, xel = (a[:, 4:6, :].rearrange("p a b -> p (a b)").rearrange("p (k s) -> p k s", k=KD) for a in (ah, al))
        yh, yl = (a[:, 6:8, :].rearrange("p a b -> p (a b)") for a in (ah, al))
        condR = sh[:, :, :].rearrange("p a (b c) -> p (a b) c", c=P)
        acc = x[:, :, TL:T]
        silu_t = lambda g: sq[:, 0, (g % 2) * 256:(g % 2 + 1) * 256]
        hh = lambda g: sq[:, 1, (g % 2) * 256:(g % 2 + 1) * 256]

        def vc(name, a=0, b=None):
            o, w = VEC[name]
            return vec[:, o + a:o + (w if b is None else b)]

        vecs_loaded, x_loaded, even_loaded, odd_loaded = map(sem, ("vecs_loaded", "x_loaded", "even_loaded", "odd_loaded"))
        landed = [sem(f"landed{i}") for i in range(SLOTS)]
        w_hi, w_lo, w_used = map(sem, ("w_hi", "w_lo", "w_used"))
        evac_act, evac_dve = sem("evac_act"), sem("evac_dve")
        sq_ready, ssq_done, root_ready, rinv_ready, t_ready = map(
            sem, ("sq_ready", "ssq_done", "root_ready", "rinv_ready", "t_ready"))
        consts_set = sem("consts_set")
        mod_h, mod_hi, mod_lo, res_done = map(sem, ("mod_h", "mod_hi", "mod_lo", "res_done"))
        cond_ready, modv_ready, scales_ready = map(sem, ("cond_ready", "modv_ready", "scales_ready"))

        evac_by = (["act"] * 2 + ["dve"] * 4 + ["act"] * 3 + ["act"] * 4 + ["dve"] * 22 + ["act"] * 10 + ["act"] * 4)

        def ordinal(s):
            if s < S_WOUT:
                return (s - MOD_FIRST) // 3
            return s - S_WOUT + WIN if s < S_DOWN else s - (S_OIN - S_DOWN) - S_WOUT + WIN

        def evacs(s, who):
            return evacs_to(ordinal(s), who)

        def evacs_to(c, who):
            return sum(w == who for w in evac_by[:c + 1])

        USED = 2 + NE * PER_EXPERT
        GROUPS = 11 * NE

        class Pass:

            def __init__(self, no):
                self.J = MOE_STREAM * no
                self.used = S_MOE + USED * no
                self.hid = (GROUPS + 1) * no
                self.turned = GROUPS * no
                self.gathered = (NE + 1) * no
                self.results = (NE + 1) * no
                self.selT = NE * no
                self.added = 1 + 4 * (NE + 1) * no

        early_landings = [S_MOE // EARLY_SLOTS] * EARLY_SLOTS + [0] * (SLOTS - EARLY_SLOTS)

        def slot(n):
            return raw[:, n * PIECE:(n + 1) * PIECE]

        block = ctx.enter_context(nc.Block())
        NK = chunks_before(len(NORMS))

        @block.sync
        def _(sp):
            sp.dma_start(vec[:, :], vec_d).then_inc(vecs_loaded, 16)
            for s in range(S_MOE):
                if s == 2:
                    sp.dma_start(x[:, :, :], x_d).then_inc(x_loaded, 16)
                    sp.dma_start(cst[:, :, :], cst_d).then_inc(sem("cst_loaded"), 16)
                if s == s_win(3):
                    sp.dma_start(rope[:, :, :], rope_d).then_inc(sem("rope_loaded"), 16)
                    sp.wait_ge(mod_lo, KD)
                    sp.dma_start(uq, uq_d).then_inc(sem("uq_loaded"), 16)
                    sp.dma_start(ukv, ukv_d).then_inc(sem("ukv_loaded"), 16)
                if s == S_OIN + 5:
                    sp.wait_ge(sem("y2_used"), 1)
                    sp.dma_start(dftc, dft_d[:, 0:256]).then_inc(sem("dftc_loaded"), 16)
                    sp.dma_start(dftt, dft_d[:, 256:1280].rearrange("p (a b) -> p a b", a=4)).then_inc(sem("dftt_loaded"), 16)
                if s >= EARLY_SLOTS:
                    sp.wait_ge(w_lo, s - EARLY_SLOTS + 1)
                sp.dma_start(slot(s % EARLY_SLOTS), w_d[s]).then_inc(landed[s % EARLY_SLOTS], 16)

            still_used = (EARLY_SLOTS, SLOTS - 1)
            for j in [j for j in range(SLOTS) if j not in still_used] + list(still_used):
                if j < EARLY_SLOTS:
                    sp.wait_ge(w_lo, S_MOE - EARLY_SLOTS + j + 1)
                if j == EARLY_SLOTS + 1:
                    sp.wait_ge(sem("o_lo"), DH)
                if j == EARLY_SLOTS:
                    sp.wait_ge(res_done, RES_BEFORE[N_O2])
                sp.dma_start(slot(j), w_d[S_MOE + j]).then_inc(landed[j], 16)

            def load(J, turns, first, tail):
                with sp.Fori(0, turns) as e:
                    for r in range(PER_EXPERT):
                        sp.wait_ge(w_lo, PER_EXPERT * e + (S_MOE + J + r - SLOTS + 1))
                        sp.dma_start(slot((J + r) % SLOTS),
                                     w_d[bass.ds(PER_EXPERT * e + (S_MOE + first + r), 1)].rearrange("o p n -> (o p) n")
                                     ).then_inc(landed[(J + r) % SLOTS], 16)
                for r in range(PER_EXPERT * turns, PER_EXPERT * turns + tail):
                    sp.wait_ge(w_lo, S_MOE + J + r - SLOTS + 1)
                    sp.dma_start(slot((J + r) % SLOTS), w_d[S_MOE + first + r]).then_inc(landed[(J + r) % SLOTS], 16)

            load(SLOTS, NE - 1, SLOTS, MOE_STREAM - SLOTS - PER_EXPERT * (NE - 1))
            sp.wait_ge(sem("count_ready"), 1)
            most = sp.value_load(cnt[0:1, 0:1], min_val=0, max_val=TL)
            with sp.If(most > P):
                load(MOE_STREAM, NE, 0, MOE_STREAM - PER_EXPERT * NE)
            for k in range(KD):
                sp.wait_ge(res_done, RES_BEFORE[N_OF] + k + 1)
                sp.dma_start(out_d[:, k, :], x[:, k, 0:TL]).then_inc(sem("stored"), 16)
            sp.wait_ge(sem("stored"), 16 * KD)

        @block.scalar
        def _(act):
            chain = [0]

            def link(ins):
                chain[0] += 1
                ins.then_inc(sem("act_chain"), 1)
                act.wait_ge(sem("act_chain"), chain[0])

            done = [0]

            def split(upto):
                while done[0] <= min(upto, S_MOE - 1):
                    s = done[0]
                    act.wait_ge(landed[s % EARLY_SLOTS], 16 * (s // EARLY_SLOTS + 1))
                    if s >= SPLITS:
                        act.wait_ge(w_used, s - SPLITS + 1)
                    act.activation(wh[:, s % SPLITS, :], slot(s % EARLY_SLOTS), ACT.Copy).then_inc(w_hi, 1)
                    done[0] += 1

            def squares(n, src, ready=None, chunks=None):
                K, W = NORMS[n]
                for k in (range(K) if chunks is None else chunks):
                    j = chunks_before(n) + k
                    if j >= 2:
                        act.wait_ge(ssq_done, j - 1)
                    if ready:
                        ready(k)
                    act.activation(sq[:, j % 2, 0:W], src(k), ACT.Square).then_inc(sq_ready, 1)

            def root(n):
                K, W = NORMS[n]
                act.wait_ge(ssq_done, chunks_before(n) + K)
                if n:
                    act.wait_ge(t_ready, chunks_before(n))
                act.activation(rinv[:, 0:W], ps[:, 4, 0:W], ACT.Ln, bias=eps[:, 0:1], scale=1.0 / NDIM[n]).then_inc(root_ready, 1)
                act.wait_ge(root_ready, n + 1)
                act.activation(rinv[:, 0:W], rinv[:, 0:W], ACT.Exp, scale=-0.5).then_inc(rinv_ready, 1)

            def modulate(n, m, layer, which, shift, dst=None, hi=True):
                K, W = NORMS[n]
                modv = (mod0, mod1)[layer]
                for k in range(K):
                    j = chunks_before(n) + k
                    act.wait_ge(t_ready, j + 1)
                    b = tmp[j % 2] if dst is None else dst(k)
                    for c in range(W // TL):
                        act.activation(b[:, c * TL:(c + 1) * TL], b[:, c * TL:(c + 1) * TL], ACT.Identity,
                                       bias=modv[:, shift + k, c:c + 1],
                                       scale=scl[:, layer, which, k, c:c + 1]).then_inc(mod_h, 1)
                    if hi:
                        act.wait_ge(mod_h, 2 * (KD * m + k + 1))
                        act.activation(ah[:, k, 0:W], b[:, 0:W], ACT.Copy).then_inc(mod_hi, 1)

            act.wait_ge(vecs_loaded, 16)
            act.activation(vc("cond"), vc("cond"), ACT.Silu).then_inc(cond_ready, 1)
            act.wait_ge(sem("cond_cleared"), 1)
            act.wait_ge(cond_ready, 1)
            act.activation(condR[:, :, 64:66], condS, ACT.Copy).then_inc(cond_ready, 1)

            def rows(n):
                act.wait_ge(w_used, s_mod(n) + 1)
                if n >= 2:
                    act.wait_ge(sem("mod_cols"), n - 1)
                act.activation(mod_row[64:68, n % 2, :], ps[64:68, 6 + n % 2, 0:256], ACT.Copy).then_inc(sem("mod_rows"), 1)

            split(1)
            rows(0)
            rows(1)
            act.wait_ge(x_loaded, 16)
            squares(N_E1, lambda k: x[:, k, :])
            act.wait_ge(sem("lam_sums"), 1)
            act.activation(small[:, 2:4], ps[:, 5, 0:2], ACT.Exp).then_inc(sem("lam_exp"), 1)
            act.wait_ge(consts_set, 1)
            split(3)
            for n in range(2, MOD_FIRST):
                split(s_mod(n) + 2)
                rows(n)
                if n == 2:
                    root(N_E1)
            act.wait_ge(scales_ready, 1)
            modulate(N_E1, 0, 0, 0, 0, lambda k: xn[:, k, :])

            for p in range(WIN + 1):
                if p:
                    for n in (MOD_FIRST + 2 * p - 2, MOD_FIRST + 2 * p - 1):
                        split(s_mod(n) + 2)
                        rows(n)
                if p == WIN:
                    break
                split(s_win(p) + 2)
                if evac_by[p] == "dve":
                    continue
                act.wait_ge(w_used, s_win(p) + 1)
                bank = 2 * (p % 2)
                dst = {0: (b_gate[:, 0, :], b_gate[:, 1, :]), 1: (b_gate[:, 2, :], b_gate[:, 3, :]),
                       6: (zq[:, 0, :], zq[:, 1, :]), 7: (zq[:, 2, :], zkv[:, 0, :]),
                       8: (zkv[:, 1, :], k_pe[0:64, :])}[p]
                n = 64 if p == 8 else P
                act.activation(dst[0], ps[:, bank, :], ACT.Copy)
                act.activation(dst[1], ps[0:n, bank + 1, :], ACT.Copy).then_inc(evac_act, 1)
            act.wait_ge(evac_act, evacs(s_win(8), "act"))
            squares(N_Q, lambda k: zq[:, k, :])
            squares(N_KV, lambda k: zkv[:, k, :])

            def filler(m):
                n = MOD_FIRST + MOD_WIN + m
                if n < N_MOD:
                    split(s_mod(n) + 2)
                    rows(n)

            root(N_Q)
            filler(0)
            for c in range(HEADS):
                act.wait_ge(sem("conv_ready"), c + 1)
                act.activation(ah[:, c, :], b_gate[:, c, :], ACT.Copy).then_inc(sem("conv_hi"), 1)
            filler(1)
            root(N_KV)
            for m in range(2, MOD_GAP):
                filler(m)

            dsts = ([(q_nope[:, h, :], P) for h in range(HEADS)] + [(q_pe[0:64, h, :], 64) for h in range(HEADS)]
                    + [(k_nope[:, h, :], P) for h in range(HEADS)] + [(v_e[:, t, :], P) for t in range(4)])
            for n, (dst, w) in enumerate(dsts):
                if n % 4 == 3:
                    filler(MOD_GAP + n // 4)
                act.wait_ge(sem("proj_ps"), n + 1)
                if n == 0:
                    act.wait_ge(sem("conv_lo"), HEADS)
                act.activation(dst, ps[0:w, n % 4, :], ACT.Copy).then_inc(sem("proj_ready"), 1)

            def attention(name, units, exp, out):
                s_ = lambda k: sem(f"{name}_{k}")
                for i in range(len(units) + 3):
                    if i < len(units):
                        act.wait_ge(s_("negmax"), i + 1)
                        if i >= 2:
                            act.wait_ge(s_("turned"), i - 1)
                        exp(i).then_inc(s_("exp"), 1)
                    if 2 <= i <= len(units) + 1:
                        u = i - 2
                        n = units[u][2]
                        act.wait_ge(s_("turned"), u + 1)
                        if u >= 2:
                            act.wait_ge(s_("pv"), u - 1)
                        pt, bank = (pt_e, 2) if name == "mla" else (pt_o, 4)
                        act.activation(pt[:, u % 2, 0:n], ps[:, bank + u % 2, 0:n], ACT.Copy).then_inc(s_("pt"), 1)
                    if i >= 3:
                        act.wait_ge(s_("pv"), i - 2)
                        out(i - 3)
                    if name == "mla":
                        filler(MOD_GAP + 4 + i)

            units = mla_units()

            def exp_e(i):
                n = units[i][2]
                return act.activation(pr_e[:, i % 2, 0:n], ps[:, i % 2, 0:n], ACT.Exp, bias=small[:, 16 + i:17 + i],
                                      scale=MLA_SCALE, accum_out=small[:, 32 + i:33 + i])

            def out_e(u):
                h, j, _, _ = units[u]
                act.activation(ah[:, HEADS + h, j * P:(j + 1) * P], ps[:, 4 + u % 2, 0:P], ACT.Copy
                               ).then_inc(sem("mla_ohi"), 1)

            attention("mla", units, exp_e, out_e)

            for p in range(4):
                s = S_WOUT + p
                split(s + 2)
                act.wait_ge(w_used, s + 1)
                bank = 2 * (ordinal(s) % 2)
                squares(N_EY, lambda k: ps[:, bank + k % 2, :], chunks=(2 * p, 2 * p + 1))
                act.activation(y_e[:, 2 * p:2 * p + 2, :], ps[:, bank:bank + 2, :], ACT.Copy).then_inc(evac_act, 1)
            root(N_EY)
            squares(N_E2, lambda k: x[:, k, :], lambda k: act.wait_ge(res_done, 2 * (k + 1)))
            root(N_E2)
            modulate(N_E2, 1, 0, 2, 24)

            for m in range(NF):
                s = S_GU + m
                split(s + 2)
                act.wait_ge(w_used, s + 1)
                if m >= 2:
                    act.wait_ge(evac_dve, evacs(s - 2, "dve"))
                act.activation(tmp[m % 2], ps[:, 2 * (ordinal(s) % 2), :], ACT.Silu).then_inc(sem("silu"), 1)

            def hidden_hi(f):
                if f >= 2:
                    if f % 2 == 0:
                        act.wait_ge(sem("f_used"), f // 2)
                    else:
                        act.wait_ge(w_used, S_DOWN + (f - 1) // 2)
                act.wait_ge(evac_dve, evacs(S_GU + f, "dve"))
                act.activation(sh[:, f % 2, :], hid[:, f, :], ACT.Copy).then_inc(sem("hid_hi"), 1)

            hidden_hi(0)
            hidden_hi(1)
            for d in range(NF // 2):
                split(S_DOWN + d + 2)
                if d + 1 < NF // 2:
                    hidden_hi(2 * d + 2)
                    hidden_hi(2 * d + 3)
            act.wait_ge(w_used, S_DOWN + NF // 2)
            act.wait_ge(sem("hid_lo"), NF)
            for q in range(2):
                squares(N_EF, lambda k: ps[:, k, :], chunks=(2 * q, 2 * q + 1))
                act.activation(y2_e[:, 2 * q:2 * q + 2, :], ps[:, 2 * q:2 * q + 2, :], ACT.Copy).then_inc(sem("y2_act"), 1)
            act.wait_ge(sem("y2_dve"), 2)
            squares(N_EF, lambda k: y2_e[:, k, :], chunks=range(4, KD))
            root(N_EF)
            squares(N_O1, lambda k: x[:, k, :], lambda k: act.wait_ge(res_done, 2 * KD + 2 * (k + 1)))
            root(N_O1)
            modulate(N_O1, 2, 1, 0, 0)

            for p in range(10):
                s = S_OIN + p
                split(s + 2)
                act.wait_ge(w_used, s + 1)
                bank = 2 * (ordinal(s) % 2)
                if p == 9:
                    act.activation(f_o[:, :, :], ps[:, bank:bank + 2, 0:TL], ACT.Copy).then_inc(evac_act, 1)
                elif p >= 6:
                    c = (p - 6) * 256
                    act.activation(v_o[:, :, c:c + 256],
                                   ps[:, bank:bank + 2, :].rearrange("p b (t n) -> p (b t) n", t=2),
                                   ACT.Copy).then_inc(evac_act, 1)
                elif p >= 3:
                    act.activation(k_o[:, 2 * p - 6:2 * p - 4, :], ps[:, bank:bank + 2, :], ACT.Copy).then_inc(evac_act, 1)
                else:
                    act.activation(q_o[:, 2 * p:2 * p + 2, :], ps[:, bank:bank + 2, 0:TL], ACT.Copy).then_inc(evac_act, 1)
            act.wait_ge(sem("four_ps"), 1)
            act.activation(mid[:, :, :].rearrange("p a b -> p (a b)"),
                           ps[:, 0:2, :].rearrange("p a b -> p (a b)"), ACT.Copy).then_inc(sem("four_mid"), 1)
            act.wait_ge(sem("four_ps"), 2)
            act.activation(ah[:, 6:8, 0:TL], ps[:, 2, :].rearrange("p (a b) -> p a b", a=2), ACT.Copy
                           ).then_inc(sem("four_hi"), 1)

            ounits = diff_units()

            def exp_o(i):
                for m in range(2):
                    ins = act.activation(pr_o[:, i % 2, m, :], ps[:, 2 * (i % 2) + m, :], ACT.Exp,
                                         bias=small[:, 16 + 2 * i + m:17 + 2 * i + m], scale=DIFF_SCALE,
                                         accum_out=small[:, 40 + 2 * i + m:41 + 2 * i + m])
                return ins

            def out_o(u):
                h, j, _, _ = ounits[u]
                act.activation(o_o[:, h, j * P:(j + 1) * P], ps[:, 6 + u % 2, 0:P], ACT.Copy).then_inc(sem("diff_out"), 1)
                if u % 4 == 1 and u > 4:
                    head_squares(u // 4 - 1)
                if u == len(ounits) - 2:
                    head_root(0, 1)

            def two_heads(v, n):
                return v[:, 2 * n:2 * n + 2, :].rearrange("p a b -> p (a b)")

            def head_squares(n):
                act.wait_ge(sem("diff_out"), 4 * n + 4)
                act.activation(two_heads(o_sq, n), two_heads(o_o, n), ACT.Square).then_inc(sem("osq_ready"), 1)

            def head_root(*groups):
                for n in groups:
                    act.wait_ge(sem("ossq_done"), n + 1)
                    act.activation(two_heads(o_rinv, n), ps[:, HEAD_SUMS[n], :], ACT.Ln, bias=eps[:, 0:1], scale=1.0 / P
                                   ).then_inc(sem("oln"), 1)
                for n in groups:
                    act.wait_ge(sem("oln"), n + 1)
                    act.activation(two_heads(o_rinv, n), two_heads(o_rinv, n), ACT.Exp, scale=-0.5).then_inc(sem("oroot"), 1)

            attention("diff", ounits, exp_o, out_o)
            head_squares(DH // 2 - 1)
            for h in range(DH):
                if h == 2:
                    head_root(DH // 2 - 1)
                act.wait_ge(sem("o_ready"), h + 1)
                act.activation(ah[:, h, 0:TL], o_o[:, h, :], ACT.Copy).then_inc(sem("o_hi"), 1)

            for p in range(4):
                s = S_OOUT + p
                split(s + 2)
                act.wait_ge(w_used, s + 1)
                bank = 2 * (ordinal(s) % 2)
                squares(N_OY, lambda k: ps[:, bank + k % 2, 0:TL], chunks=(2 * p, 2 * p + 1))
                act.activation(y_o[:, 2 * p:2 * p + 2, :], ps[:, bank:bank + 2, 0:TL], ACT.Copy).then_inc(evac_act, 1)
            root(N_OY)
            squares(N_O2, lambda k: x[:, k, 0:TL], lambda k: act.wait_ge(res_done, 4 * KD + k + 1))
            root(N_O2)
            modulate(N_O2, 3, 1, 2, 24, lambda k: h2f[:, k, :], hi=False)

            act.wait_ge(sem("top_diff"), 1)
            act.activation(small[:, 4:6], small[:, 2:4], ACT.Exp).then_inc(sem("top_exp"), 1)
            for t in range(2):
                act.wait_ge(sem("tok_ps"), t + 1)
                act.activation(h2h[:, t, :], ps[:, 2 * t:2 * t + 2, :].rearrange("p a b -> p (a b)"), ACT.Copy
                               ).then_inc(sem("tok_hi"), 1)

            def gathered(idx):
                act.wait_ge(sem("xh_ps"), idx)
                act.activation(xeh[:, :, :].rearrange("p a b -> p (a b)"),
                               ps[:, 6:8, :].rearrange("p a b -> p (a b)"), ACT.Copy).then_inc(sem("xe_h"), 1)

            def experts(no):
                at = Pass(no)

                def split_next(e, j):
                    J = at.J + j
                    act.wait_ge(landed[J % SLOTS], 3 * 16 * e + 16 * (early_landings[J % SLOTS] + J // SLOTS + 1))
                    act.wait_ge(w_used, PER_EXPERT * e + at.used + max(j - SPLITS + 1, 0))
                    act.activation(wh[:, J % SPLITS, :], slot(J % SLOTS), ACT.Copy).then_inc(w_hi, 1)

                def silu(g, used):
                    act.wait_ge(w_used, used)
                    gu = ps[:, g % 2, :].rearrange("p (b w c) -> p b w c", b=2, w=2)
                    act.activation(silu_t(g).rearrange("p (b c) -> p b c", b=2), gu[:, :, 0, :], ACT.Silu
                                   ).then_inc(sem("moe_silu"), 1)

                def hidden_hi(e, g):
                    act.wait_ge(sem("hid_T"), 11 * e + (at.hid + g + 1))
                    act.activation(sh[:, g % 2, 0:256], ps[:, 5, 0:256], ACT.Copy).then_inc(sem("hT_hi"), 1)

                def result_hi(e):
                    act.wait_ge(w_used, PER_EXPERT * e + at.used + 2)
                    act.activation(yh, ps[:, 3:5, :].rearrange("p a b -> p (a b)"), ACT.Copy, scale=gslot
                                   ).then_inc(sem("y_h"), 1)

                act.wait_ge(w_lo, S_MOE + at.J)
                for j in range(AHEAD):
                    split_next(0, j)
                gathered(at.gathered + 1)
                split_next(0, AHEAD)
                silu(0, at.used + 2)
                split_next(0, AHEAD + 1)
                act.wait_ge(sem("y_clear"), 3 * (no + 1))
                with act.Fori(0, NE) as e:
                    result_hi(e)
                    hidden_hi(e, 0)
                    for q, (kind, g, half) in enumerate(ORDER):
                        if kind == "gu" and half == 1:
                            silu(g, PER_EXPERT * e + (at.used + 2 + q + 1))
                        if q == GATHER + 1:
                            gathered(e + (at.gathered + 2))
                        split_next(e, 2 + q + AHEAD)
                        if TURN.get(q):
                            hidden_hi(e, TURN[q])
                        if q == 5:
                            act.wait_ge(sem("selT_ps"), e + (at.selT + 1))
                            act.activation(selT, ps[:, 2, 0:TL], ACT.Copy)
                            act.activation(gslot, ps[:, 2, TL:TL + 1], ACT.Copy).then_inc(sem("selT_ready"), 1)
                result_hi(NE)

            experts(0)
            act.wait_ge(sem("count_ready"), 1)
            most = act.value_load(cnt[0:1, 0:1], min_val=0, max_val=TL)
            with act.If(most > P):
                experts(1)
            squares(N_OF, lambda k: acc[:, k, :], lambda k: act.wait_ge(sem("acc_final"), 1))
            root(N_OF)

        @block.vector
        def _(dve):
            chain = [0]

            def link(ins):
                chain[0] += 1
                ins.then_inc(sem("dve_chain"), 1)
                dve.wait_ge(sem("dve_chain"), chain[0])

            done = [0]

            def split(upto):
                while done[0] <= min(upto, S_MOE - 1):
                    s = done[0]
                    dve.wait_ge(w_hi, s + 1)
                    dve.tensor_tensor(wl[:, s % SPLITS, :], slot(s % EARLY_SLOTS), wh[:, s % SPLITS, :].bitcast(F32),
                                      ALU.subtract).then_inc(w_lo, 1)
                    done[0] += 1

            def inverse(n):
                dve.wait_ge(rinv_ready, n + 1)

            def normed(n, src, dst, k):
                dve.tensor_tensor(dst, src, rinv[:, 0:NORMS[n][1]], ALU.mult).then_inc(t_ready, 1)

            def modulate(n, m, dst=None):
                K, W = NORMS[n]
                inverse(n)
                dve.wait_ge(res_done, RES_BEFORE[n])
                for k in range(K + 1):
                    if k < K:
                        j = chunks_before(n) + k
                        if k >= 2 and dst is None:
                            dve.wait_ge(mod_lo, KD * m + k - 1)
                        normed(n, x[:, k, 0:W], tmp[j % 2] if dst is None else dst(k), k)
                    if k and dst is None:
                        j = chunks_before(n) + k - 1
                        dve.wait_ge(mod_hi, KD * m + k)
                        dve.tensor_tensor(al[:, k - 1, 0:W], tmp[j % 2][:, 0:W], ah[:, k - 1, 0:W].bitcast(F32),
                                          ALU.subtract).then_inc(mod_lo, 1)

            def residual(n, src, layer, which):
                K, W = NORMS[n]
                inverse(n)
                for k in range(K + 1):
                    if k < K:
                        j = chunks_before(n) + k
                        if k >= 2:
                            dve.wait_ge(res_done, RES_BEFORE[n] + (W // TL) * (k - 1))
                        normed(n, src(k), tmp[j % 2][:, 0:W], k)
                    if k:
                        j = chunks_before(n) + k - 1
                        dve.wait_ge(t_ready, j + 1)
                        for c in range(W // TL):
                            dve.scalar_tensor_tensor(
                                out=x[:, k - 1, c * TL:(c + 1) * TL], in0=tmp[j % 2][:, c * TL:(c + 1) * TL],
                                scalar=scl[:, layer, which, k - 1, c:c + 1], in1=x[:, k - 1, c * TL:(c + 1) * TL],
                                op0=ALU.mult, op1=ALU.add).then_inc(res_done, 1)

            def flat(v):
                return v.rearrange("p a b -> p (a b)")

            def take_modulation(layer, lo, hi):
                modv = (mod0, mod1)[layer][:, 2 * lo:2 * hi, :].rearrange("p (i a c) s -> p i a c s", a=2, c=2)
                bias = vc(f"mod_b{layer}", 4 * lo, 4 * hi).rearrange("p (i a c s) -> p i a c s", a=2, c=2, s=2)
                c0 = 256 + 96 * layer + 4 * lo
                for a in range(2):
                    part = ps[:, 6 + a, c0:c0 + 4 * (hi - lo)].rearrange("p (i c h s) -> p i c h s", c=2, h=2, s=2)
                    for c in range(2):
                        link(dve.tensor_tensor(modv[:, :, a, c, :], part[:, :, c, 0, :], bias[:, :, a, c, :], ALU.add))
                        link(dve.tensor_tensor(modv[:, :, a, c, :], part[:, :, c, 1, :], modv[:, :, a, c, :], ALU.add))

            def scale_pre(layer, which, chunk):
                modv = (mod0, mod1)[layer]
                return dve.scalar_tensor_tensor(out=flat(scl[:, layer, which, :, :]), in0=flat(modv[:, chunk:chunk + KD, :]),
                                                scalar=1.0, in1=vc(f"norm{layer}", 16 * which, 16 * which + 16),
                                                op0=ALU.add, op1=ALU.mult)

            def scale_post(layer, which, chunk):
                modv = (mod0, mod1)[layer]
                return dve.tensor_tensor(flat(scl[:, layer, which, :, :]), flat(modv[:, chunk:chunk + KD, :]),
                                         vc(f"norm{layer}", 16 * which, 16 * which + 16), ALU.mult)

            dve.memset(condR.bitcast(F32), 0.0).then_inc(sem("cond_cleared"), 1)
            dve.memset(eps[:, :], EPS).then_inc(consts_set, 1)
            link(dve.memset(flat(area(4096, HEADS * 2, 258)), 0.0))
            dve.wait_ge(vecs_loaded, 16)
            lam = vc("lam").rearrange("p (a b) -> p a b", b=2)
            dve.tensor_tensor(small[0:64, 0:2], lam[0:64, :, 0], lam[0:64, :, 1], ALU.mult).then_inc(sem("lam_prod"), 1)
            dve.wait_ge(cond_ready, 2)
            dve.wait_ge(sem("cond_cleared"), 1)
            dve.tensor_tensor(condR[:, :, 66:68], condS, condR[:, :, 64:66].bitcast(F32), ALU.subtract).then_inc(sem("cond_split"), 1)
            split(4)
            dve.wait_ge(sem("lam_exp"), 1)
            link(dve.tensor_tensor(small[:, 6:7], small[:, 3:4], small[:, 2:3], ALU.subtract))
            link(dve.tensor_scalar(small[:, 7:8], small[:, 6:7], -LAM_INIT, None, ALU.add))
            link(dve.tensor_scalar(small[:, 8:9], vc("subln"), 1.0 - LAM_INIT, None, ALU.mult))
            inverse(N_E1)
            for k in range(KD):
                normed(N_E1, x[:, k, :], xn[:, k, :], k)
                split(5 + k // 2)
            split(MOD_FIRST + 1)
            dve.wait_ge(sem("mod_cols"), MOD_FIRST)
            take_modulation(0, 0, MOD_FIRST)
            scale_pre(0, 0, 8).then_inc(scales_ready, 1)
            for k in range(KD):
                dve.wait_ge(mod_hi, k + 1)
                dve.tensor_tensor(al[:, k, :], xn[:, k, :], ah[:, k, :].bitcast(F32), ALU.subtract).then_inc(mod_lo, 1)

            def conv(c):
                t = tmp[c % 2].rearrange("p (s t) -> p s t", s=2)
                w = lambda j: vc("conv", 4 * j + c, 4 * j + c + 1)
                if c == 0:
                    dve.wait_ge(evac_dve, evacs(s_win(8), "dve"))
                    dve.wait_ge(evac_act, evacs(s_win(1), "act"))
                if c >= 2:
                    dve.wait_ge(sem("conv_ready"), c - 1)
                link(dve.tensor_scalar(t, cu[:, c, :, 1:257], w(1), None, ALU.mult))
                for j in (0, 2):
                    link(dve.scalar_tensor_tensor(out=t, in0=cu[:, c, :, j:j + 256], scalar=w(j), in1=t,
                                                  op0=ALU.mult, op1=ALU.add))
                dve.tensor_tensor(b_gate[:, c, :], tmp[c % 2], b_gate[:, c, :], ALU.mult).then_inc(sem("conv_ready"), 1)

            for p in range(WIN + 1):
                if p:
                    split(s_win(p) + 1)
                if p == WIN:
                    conv(3)
                    break
                split(s_win(p) + 2)
                if p > 5:
                    conv(p - 6)
                if evac_by[p] == "act":
                    continue
                dve.wait_ge(w_used, s_win(p) + 1)
                if p >= 4:
                    dve.wait_ge(evac_dve, p - 3)
                else:
                    dve.wait_ge(mod_lo, KD)
                bank = 2 * (p % 2)
                dve.tensor_copy(tmp[p % 2], ps[:, bank, :]).then_inc(sem("c_copied"), 1)
                dve.wait_ge(sem("c_copied"), p - 1)
                dve.tensor_tensor(cu[:, p - 2, :, 1:257], ps[:, bank + 1, :].rearrange("p (s t) -> p s t", s=2),
                                  tmp[p % 2].rearrange("p (s t) -> p s t", s=2), ALU.mult).then_inc(evac_dve, 1)
            inverse(N_Q)
            dve.wait_ge(evac_act, evacs(s_win(8), "act"))
            for k in range(QR):
                dve.scalar_tensor_tensor(out=zq[:, k, :], in0=zq[:, k, :], scalar=vc("qn", k, k + 1), in1=rinv[:, :],
                                         op0=ALU.mult, op1=ALU.mult).then_inc(t_ready, 1)

            def filler(m):
                if MOD_FIRST + MOD_WIN + m < N_MOD:
                    split(s_mod(MOD_FIRST + MOD_WIN + m) + 2)

            filler(0)
            def conv_lo(c):
                dve.wait_ge(sem("conv_hi"), c + 1)
                dve.tensor_tensor(al[:, c, :], b_gate[:, c, :], ah[:, c, :].bitcast(F32), ALU.subtract).then_inc(sem("conv_lo"), 1)

            dve.wait_ge(w_used, s_win(WIN - 1) + 1)
            for c in range(HEADS):
                conv_lo(c)
            filler(1)
            inverse(N_KV)
            for k in range(KVR):
                dve.scalar_tensor_tensor(out=zkv[:, k, :], in0=zkv[:, k, :], scalar=vc("kvn", k, k + 1), in1=rinv[:, :],
                                         op0=ALU.mult, op1=ALU.mult).then_inc(t_ready, 1)
            for m in range(2, MOD_GAP):
                filler(m)
            cosb, sinb = rope[:, 0, :], rope[:, 1, :]

            def rotate(dst, turned, w, signal, buf, heads):
                t = tmp[buf][0:w, 0:heads * TL].rearrange("p (h t) -> p h t", h=heads)
                for h in range(heads):
                    dve.tensor_tensor(t[:, h, :], turned[:, h, :], sinb[0:w, :], ALU.mult)
                    ins = dve.tensor_tensor(dst[:, h, :], dst[:, h, :], cosb[0:w, :], ALU.mult)
                link(ins)
                dve.tensor_tensor(dst, dst, t, ALU.add).then_inc(signal, 1)

            dve.wait_ge(sem("rope_loaded"), 16)
            dve.wait_ge(sem("conv_lo"), HEADS)
            dve.wait_ge(sem("rope_ps"), 1)
            rotate(k_pe[0:64, None, 0:TL], ps[0:64, 5, None, 0:TL], 64, sem("rope_done"), 0, 1)

            for m in range(3):
                filler(MOD_GAP + m)
            for g in range(2):
                dve.wait_ge(sem("rope_ps"), g + 2)
                rotate(q_pe[0:64, 2 * g:2 * g + 2, 0:TL], ps[0:64, 4 + g, :].rearrange("p (h t) -> p h t", h=2), 64,
                       sem("rope_done"), 1 - g, 2)

            def attention(name, units, scale, scaled, out):
                s_ = lambda k: sem(f"{name}_{k}")
                nm = 1 if name == "mla" else 2
                sums = 32 if name == "mla" else 40
                for i in range(len(units) + 3):
                    if i < len(units):
                        n = units[i][2]
                        dve.wait_ge(s_("scores"), i + 1)
                        cols = slice(16 + nm * i, 16 + nm * (i + 1))
                        if nm == 1:
                            src = ps[:, i % 2, 0:n]
                        else:
                            src = ps[:, 2 * (i % 2):2 * (i % 2) + 2, :]
                        link(dve.tensor_reduce(small[:, cols], src, AX.X, ALU.max))
                        dve.tensor_scalar(small[:, cols], small[:, cols], -scale, None, ALU.mult).then_inc(s_("negmax"), 1)
                    if i >= 3:
                        out(i - 3)
                    if 1 <= i <= len(units):
                        u = i - 1
                        dve.wait_ge(s_("exp"), u + 1)
                        cols = slice(sums + nm * u, sums + nm * (u + 1))
                        link(dve.reciprocal(small[:, cols], small[:, cols]))
                        scaled(u).then_inc(s_("probs"), 1)
                    if name == "mla":
                        filler(MOD_GAP + 4 + i)

            units = mla_units()

            def scaled_e(i):
                n = units[i][2]
                return dve.tensor_scalar(pr_e[:, i % 2, 0:n], pr_e[:, i % 2, 0:n], small[:, 32 + i:33 + i], None, ALU.mult)

            def out_e(u):
                h, j, _, _ = units[u]
                cols = slice(j * P, (j + 1) * P)
                dve.wait_ge(sem("mla_ohi"), u + 1)
                dve.tensor_tensor(al[:, HEADS + h, cols], ps[:, 4 + u % 2, 0:P], ah[:, HEADS + h, cols].bitcast(F32),
                                  ALU.subtract).then_inc(sem("mla_out"), 1)

            filler(MOD_GAP + 3)
            attention("mla", units, MLA_SCALE, scaled_e, out_e)
            dve.wait_ge(sem("mod_cols"), N_MOD)
            take_modulation(0, MOD_FIRST, 24)
            link(scale_post(0, 1, 16))
            link(scale_pre(0, 2, 32))
            link(scale_post(0, 3, 40))
            take_modulation(1, 0, 24)
            link(scale_pre(1, 0, 8))
            link(scale_post(1, 1, 16))
            link(scale_pre(1, 2, 32))
            scale_post(1, 3, 40).then_inc(scales_ready, 1)

            split(S_WOUT + 5)
            dve.wait_ge(evac_act, evacs(S_WOUT + 3, "act"))
            residual(N_EY, lambda k: y_e[:, k, :], 0, 1)
            modulate(N_E2, 1)
            for m in range(NF):
                s = S_GU + m
                split(s + 2)
                dve.wait_ge(sem("silu"), m + 1)
                dve.tensor_tensor(hid[:, m, :], tmp[m % 2], ps[:, 2 * (ordinal(s) % 2) + 1, :], ALU.mult).then_inc(evac_dve, 1)

            def hidden_lo(f):
                dve.wait_ge(sem("hid_hi"), f + 1)
                dve.tensor_tensor(sl[:, f % 2, :], hid[:, f, :], sh[:, f % 2, :].bitcast(F32), ALU.subtract
                                  ).then_inc(sem("hid_lo"), 1)

            hidden_lo(0)
            hidden_lo(1)
            for d in range(NF // 2):
                split(S_DOWN + d + 2)
                if d + 1 < NF // 2:
                    hidden_lo(2 * d + 2)
                    hidden_lo(2 * d + 3)
            dve.wait_ge(w_used, S_DOWN + NF // 2)
            for q in range(2, 4):
                dve.tensor_copy(y2_e[:, 2 * q:2 * q + 2, :], ps[:, 2 * q:2 * q + 2, :]).then_inc(sem("y2_dve"), 1)
            dve.wait_ge(sem("y2_act"), 2)
            dve.wait_ge(sem("y2_dve"), 2)
            residual(N_EF, lambda k: y2_e[:, k, :], 0, 3)
            dve.wait_ge(res_done, 4 * KD)
            dve.memset(small[:, 9:10], 0.0).then_inc(sem("y2_used"), 1)
            modulate(N_O1, 2)

            for p in range(10):
                split(S_OIN + p + 2)
                if 1 <= p <= 6:
                    dve.wait_ge(sem("orope_ps"), p)
                    dst = q_o[:, 2 * p - 2:2 * p, :] if p <= 3 else k_o[:, 2 * p - 8:2 * p - 6, 0:TL]
                    rotate(dst, ps[:, 4 + p % 2, :].rearrange("p (h t) -> p h t", h=2), P, sem("orope_done"), p % 2, 2)
            dve.wait_ge(sem("four_hi"), 1)
            dve.tensor_tensor(al[:, 6:8, 0:TL], ps[:, 2, :].rearrange("p (a b) -> p a b", a=2),
                              ah[:, 6:8, 0:TL].bitcast(F32), ALU.subtract).then_inc(sem("four_lo"), 1)

            ounits = diff_units()

            def scaled_o(i):
                at = 40 + 2 * i
                link(dve.tensor_scalar(small[:, at + 1:at + 2], small[:, at + 1:at + 2], small[:, 7:8], None, ALU.mult))
                link(dve.tensor_scalar(pr_o[:, i % 2, 0, :], pr_o[:, i % 2, 0, :], small[:, at:at + 1], None, ALU.mult))
                return dve.scalar_tensor_tensor(out=pr_o[:, i % 2, 0, :], in0=pr_o[:, i % 2, 1, :],
                                                scalar=small[:, at + 1:at + 2], in1=pr_o[:, i % 2, 0, :],
                                                op0=ALU.mult, op1=ALU.add)

            attention("diff", ounits, DIFF_SCALE, scaled_o, lambda u: None)
            for h in range(DH + 1):
                if h % 2 == 0 and h < DH:
                    dve.wait_ge(sem("oroot"), h // 2 + 1)
                if h < DH:
                    dve.scalar_tensor_tensor(out=o_o[:, h, :], in0=o_o[:, h, :], scalar=small[:, 8:9],
                                             in1=o_rinv[:, h, :], op0=ALU.mult, op1=ALU.mult).then_inc(sem("o_ready"), 1)
                if h:
                    dve.wait_ge(sem("o_hi"), h)
                    dve.tensor_tensor(al[:, h - 1, 0:TL], o_o[:, h - 1, :], ah[:, h - 1, 0:TL].bitcast(F32), ALU.subtract
                                      ).then_inc(sem("o_lo"), 1)
            split(S_OOUT + 3)
            dve.wait_ge(evac_act, evacs(S_OOUT + 3, "act"))
            residual(N_OY, lambda k: y_o[:, k, :], 1, 1)
            modulate(N_O2, 3, lambda k: h2f[:, k, :])

            def two(at):
                return small[:, at:at + 2]

            def eight(at):
                return small[:, at:at + 16].rearrange("p (t e) -> p t e", t=2)

            L, oh, oh2, t_, gates = eight(16), eight(32), eight(48), eight(64), eight(80)
            v1, v2, idx = two(10), two(12), two(14)
            iota8 = iota[:, 0:NE]
            dve.wait_ge(sem("logits_ps"), 1)
            link(dve.tensor_copy(flat(L), ps[:, 4, 0:16]))

            def pick(values, best, onehot):
                link(dve.tensor_reduce(best, values, AX.X, ALU.max))
                for t in range(2):
                    ins = dve.tensor_scalar(t_[:, t, :], values[:, t, :], best[:, t:t + 1], None, ALU.is_equal)
                link(ins)
                for t in range(2):
                    ins = dve.scalar_tensor_tensor(out=t_[:, t, :], in0=t_[:, t, :], scalar=-float(NE), in1=iota8,
                                                   op0=ALU.mult, op1=ALU.add)
                link(ins)
                link(dve.tensor_reduce(idx, t_, AX.X, ALU.min))
                for t in range(2):
                    ins = dve.tensor_scalar(onehot[:, t, :], t_[:, t, :], idx[:, t:t + 1], None, ALU.is_equal)
                link(ins)

            pick(L, v1, oh)
            link(dve.scalar_tensor_tensor(out=flat(L), in0=flat(oh), scalar=-3.0e38, in1=flat(L), op0=ALU.mult, op1=ALU.add))
            pick(L, v2, oh2)
            dve.tensor_tensor(small[:, 2:4], v2, v1, ALU.subtract).then_inc(sem("top_diff"), 1)
            dve.wait_ge(sem("top_exp"), 1)
            link(dve.tensor_scalar(v1, small[:, 4:6], 1.0, None, ALU.add))
            link(dve.reciprocal(v1, v1))
            link(dve.tensor_tensor(v2, small[:, 4:6], v1, ALU.mult))
            for t in range(2):
                ins = dve.tensor_scalar(gates[:, t, :], oh[:, t, :], v1[:, t:t + 1], None, ALU.mult)
            link(ins)
            for t in range(2):
                ins = dve.scalar_tensor_tensor(out=gates[:, t, :], in0=oh2[:, t, :], scalar=v2[:, t:t + 1],
                                               in1=gates[:, t, :], op0=ALU.mult, op1=ALU.add)
            link(ins)
            dve.tensor_tensor(flat(oh), flat(oh), flat(oh2), ALU.add).then_inc(sem("mask_ready"), 1)
            link(dve.memset(flat(rg[:, :, :]), -1.0))
            for t in range(2):
                ins = dve.tensor_copy(rg[:, 0:NE, 2 + t], gates[:, t, :])
            dve.wait_ge(sem("rank_ps"), 1)
            link(dve.scalar_tensor_tensor(out=flat(t_), in0=ps[:, 4, 16:32], scalar=1.0, in1=flat(oh), op0=ALU.add, op1=ALU.mult))
            for t in range(2):
                ins = dve.tensor_scalar(rg[:, 0:NE, t], t_[:, t, :], -1.0, None, ALU.add)
            link(ins)
            dve.tensor_reduce(cnt[:, :], ps[:, 4, 32:40], AX.X, ALU.max).then_inc(sem("count_ready"), 1)
            for t in range(2):
                dve.wait_ge(sem("tok_hi"), t + 1)
                dve.tensor_tensor(h2l[:, t, :], ps[:, 2 * t:2 * t + 2, :].rearrange("p a b -> p (a b)"),
                                  h2h[:, t, :].bitcast(F32), ALU.subtract).then_inc(sem("tok_lo"), 1)
            dve.wait_ge(sem("tok_ps"), 2)
            dve.memset(acc, 0.0).then_inc(sem("acc_done"), 1)

            def select(e):
                link_in_loop(dve.tensor_copy(cur, rg[:, bass.ds(e, 1), :].rearrange("p o c -> p (o c)")))
                for t in range(2):
                    ins = dve.tensor_scalar(sel[:, t, :], iota, cur[:, t:t + 1], None, ALU.is_equal)
                ins.then_inc(sem("sel_ready"), 1)

            cur_count = [None]

            def link_in_loop(ins):
                ins.then_inc(sem("cur_ready"), 1)
                dve.wait_ge(sem("cur_ready"), cur_count[0])

            def gathered(idx):
                dve.wait_ge(sem("xl_ps"), idx)
                dve.tensor_copy(flat(xel[:, :, :]), ps[:, 1:3, :].rearrange("p a b -> p (a b)")).then_inc(sem("xe_l"), 1)

            def experts(no):
                at = Pass(no)

                def split_next(e, j):
                    J = at.J + j
                    dve.wait_ge(w_hi, PER_EXPERT * e + (S_MOE + J + 1))
                    dve.tensor_tensor(wl[:, J % SPLITS, :], slot(J % SLOTS), wh[:, J % SPLITS, :].bitcast(F32),
                                      ALU.subtract).then_inc(w_lo, 1)

                def hidden(g, count):
                    dve.wait_ge(sem("moe_silu"), count)
                    gu = ps[:, g % 2, :].rearrange("p (b w c) -> p b w c", b=2, w=2)
                    dve.tensor_tensor(hh(g).rearrange("p (b c) -> p b c", b=2), silu_t(g).rearrange("p (b c) -> p b c", b=2),
                                      gu[:, :, 1, :], ALU.mult).then_inc(sem("moe_hid"), 1)

                def hidden_lo(e, g):
                    dve.wait_ge(sem("hT_hi"), 11 * e + (at.turned + g + 1))
                    dve.tensor_tensor(sl[:, g % 2, 0:256], ps[:, 5, 0:256], sh[:, g % 2, 0:256].bitcast(F32),
                                      ALU.subtract).then_inc(sem("hT_lo"), 1)

                def result_lo(e):
                    dve.wait_ge(sem("y_h"), e + (at.results + 1))
                    dve.scalar_tensor_tensor(out=yl, in0=ps[:, 3:5, :].rearrange("p a b -> p (a b)"), scalar=gslot,
                                             in1=yh.bitcast(F32), op0=ALU.mult, op1=ALU.subtract).then_inc(sem("y_l"), 1)

                def add(e):
                    for c in range(4):
                        dve.wait_ge(sem("scat_ps"), 4 * e + (at.added + c))
                        dve.tensor_tensor(acc[:, 2 * c:2 * c + 2, :], acc[:, 2 * c:2 * c + 2, :],
                                          ps[:, SCATTER[c], :].rearrange("p (a b) -> p a b", a=2), ALU.add
                                          ).then_inc(sem("acc_done"), 1)

                dve.wait_ge(sem("acc_done"), at.added)
                if no:
                    dve.wait_ge(sem("y_l"), at.results)
                else:
                    dve.wait_ge(sem("tok_lo"), 2)
                    dve.wait_ge(sem("count_ready"), 1)
                dve.memset(selT.bitcast(F32), 0.0).then_inc(sem("y_clear"), 1)
                dve.memset(gslot, 0.0).then_inc(sem("y_clear"), 1)
                dve.memset(ps[:, 3:5, :], 0.0).then_inc(sem("y_clear"), 1)
                cur_count[0] = at.gathered + 1
                select(0)
                for j in range(AHEAD):
                    split_next(0, j)
                gathered(at.gathered + 1)
                split_next(0, AHEAD)
                hidden(0, at.hid + 1)
                split_next(0, AHEAD + 1)
                with dve.Fori(0, NE) as e:
                    result_lo(e)
                    hidden_lo(e, 0)
                    for q, (kind, g, half) in enumerate(ORDER):
                        if q == 1:
                            add(e)
                        if kind == "gu" and half == 1:
                            hidden(g, 11 * e + (at.hid + (g or 11) + 1))
                        split_next(e, 2 + q + AHEAD)
                        if TURN.get(q):
                            hidden_lo(e, TURN[q])
                        if q == 24:
                            dve.wait_ge(sem("selT_ps"), e + (at.selT + 1))
                            cur_count[0] = e + (at.gathered + 2)
                            select(e + 1)
                        if q == GATHER:
                            gathered(e + (at.gathered + 2))
                result_lo(NE)
                add(NE)

            experts(0)
            dve.wait_ge(sem("count_ready"), 1)
            most = dve.value_load(cnt[0:1, 0:1], min_val=0, max_val=TL)
            with dve.If(most > P):
                dve.tensor_scalar(rg[:, :, 0:2], rg[:, :, 0:2], -float(P), None, ALU.add).then_inc(sem("ranks_moved"), 1)
                dve.wait_ge(sem("ranks_moved"), 1)
                experts(1)
            dve.memset(small[:, 0:1], 0.0).then_inc(sem("acc_final"), 1)
            residual(N_OF, lambda k: acc[:, k, :], 1, 3)

        @block.tensor
        def _(pe):
            def mm3(out, lh, ll, rh, rl, start, stop):
                pe.matmul(out, lh, rh, start=start, stop=False)
                pe.matmul(out, lh, rl, start=False, stop=False)
                return pe.matmul(out, ll, rh, start=False, stop=stop)

            def sum_squares(n, chunks=None):
                K, W = NORMS[n]
                if n:
                    pe.wait_ge(root_ready, n)
                for k in (range(K) if chunks is None else chunks):
                    j = chunks_before(n) + k
                    pe.wait_ge(sq_ready, j + 1)
                    pe.matmul(ps[:, 4, 0:W], ones, sq[:, j % 2, 0:W], start=(k == 0), stop=(k == K - 1)
                              ).then_inc(ssq_done, 1)

            def out_pieces(first, W, n, ready=None):
                for p in range(4):
                    piece(first + p, W, None if p else ready)
                    if p:
                        sum_squares(n, (2 * p - 2, 2 * p - 1))
                sum_squares(n, (6, 7))

            def mod_piece(n):
                s = s_mod(n)
                pe.wait_ge(w_lo, s + 1)
                if n >= 2:
                    pe.wait_ge(sem("mod_rows"), n - 1)
                for k in range(KD):
                    for w in (wh, wl):
                        mm = pe.matmul(ps[:, 6 + n % 2, 0:256], condR[:, k, :], w[:, s % SPLITS, k * 256:(k + 1) * 256],
                                       start=(k == 0 and w is wh), stop=(k == KD - 1 and w is wl))
                mm.then_inc(w_used, 1)

            def mod_cols(n):
                pe.wait_ge(sem("mod_rows"), n + 1)
                for c in range(2):
                    at = 256 + 96 * (n // 24) + 8 * (n % 24 // 2) + 4 * c
                    mm = pe.matmul(ps[:, 6 + n % 2, at:at + 4], mod_row[64:68, n % 2, c * P:(c + 1) * P],
                                   ident[64:68, 64:68], start=True, stop=True)
                mm.then_inc(sem("mod_cols"), 1)

            def piece(s, W, first=None, widths=(P, P), tokens=False):
                pe.wait_ge(w_lo, s + 1)
                c0 = ordinal(s)
                if c0 >= 2:
                    for who, taken in (("act", evac_act), ("dve", evac_dve)):
                        if evacs_to(c0 - 2, who):
                            pe.wait_ge(taken, evacs_to(c0 - 2, who))
                bank = 2 * (c0 % 2)
                b = s % SPLITS
                if tokens:
                    for t in range(4):
                        for k in range(KD):
                            mm = mm3(ps[:, bank + t // 2, (t % 2) * 256:(t % 2) * 256 + 256],
                                     ah[:, k, t * P:(t + 1) * P], al[:, k, t * P:(t + 1) * P],
                                     wh[:, b, k * 256:(k + 1) * 256], wl[:, b, k * 256:(k + 1) * 256],
                                     k == 0, k == KD - 1)
                else:
                    for c in range(2):
                        for k in range(KD):
                            if first and c == 0:
                                first(k)
                            at = k * 256 + c * P
                            mm = mm3(ps[:, bank + c, 0:W], wh[:, b, at:at + P], wl[:, b, at:at + P],
                                     ah[:, k, 0:W], al[:, k, 0:W], k == 0, k == KD - 1)
                mm.then_inc(w_used, 1)

            pe.wait_ge(sem("cond_split"), 1)
            mod_piece(0)
            mod_piece(1)
            pe.wait_ge(sem("cst_loaded"), 16)
            pe.wait_ge(sem("lam_prod"), 1)
            pe.matmul(ps[:, 5, 0:2], ones[0:64, :], small[0:64, 0:2], start=True, stop=True).then_inc(sem("lam_sums"), 1)
            mod_cols(0)
            sum_squares(N_E1)
            for n in range(2, MOD_FIRST):
                mod_cols(n - 1)
                mod_piece(n)
            mod_cols(MOD_FIRST - 1)
            for p in range(WIN):
                piece(s_win(p), T, (lambda k: pe.wait_ge(mod_lo, k + 1)) if p == 0 else None)
                for n in (MOD_FIRST + 2 * p, MOD_FIRST + 2 * p + 1):
                    mod_piece(n)
                    if n > MOD_FIRST:
                        mod_cols(n - 1)
            sum_squares(N_Q)
            sum_squares(N_KV)

            def filler(m):
                if MOD_FIRST + MOD_WIN + m < N_MOD:
                    mod_piece(MOD_FIRST + MOD_WIN + m)
                    mod_cols(MOD_FIRST + MOD_WIN + m - 1)

            for m in range(MOD_GAP):
                filler(m)

            jobs = []
            for h in range(HEADS):
                jobs.append((P, [(uq[:, k, h * 192:h * 192 + P], zq[:, k, :]) for k in range(QR)]))
            for h in range(HEADS):
                jobs.append((64, [(uq[:, k, h * 192 + P:h * 192 + 192], zq[:, k, :]) for k in range(QR)]))
            for h in range(HEADS):
                jobs.append((P, [(ukv[:, k, h * 256:h * 256 + P], zkv[:, k, :]) for k in range(KVR)]))
            for t in range(4):
                jobs.append((P, [(zkv[:, k, t * P:(t + 1) * P],
                                  ukv[:, k, :].rearrange("p (h c) -> p h c", h=HEADS)[:, :, P:256]) for k in range(KVR)]))
            pe.wait_ge(sem("uq_loaded"), 16)
            pe.wait_ge(sem("ukv_loaded"), 16)
            pe.wait_ge(t_ready, chunks_before(N_KV))
            pe.wait_ge(evac_act, evacs(s_win(8), "act"))
            pe.wait_ge(evac_dve, evacs(s_win(8), "dve"))
            pe.matmul(ps[0:64, 5, 0:TL], rot[0:64, 0:64], k_pe[0:64, 0:TL], start=True, stop=True).then_inc(sem("rope_ps"), 1)
            for n, (w, parts) in enumerate(jobs):
                if n >= 4:
                    pe.wait_ge(sem("proj_ready"), n - 3)
                if n == 2 * HEADS:
                    pe.wait_ge(t_ready, chunks_before(N_KV) + KVR)
                for k, (l, r) in enumerate(parts):
                    mm = pe.matmul(ps[0:w, n % 4, :], l, r, start=(k == 0), stop=(k == len(parts) - 1))
                mm.then_inc(sem("proj_ps"), 1)
                if n % 4 == 3:
                    filler(MOD_GAP + n // 4)
                if n == 11:
                    pe.wait_ge(sem("rope_done"), 1)
                    pe.wait_ge(root_ready, N_KV + 1)
                    for g in range(2):
                        pe.matmul(ps[0:64, 4 + g, :], rot[0:64, 0:64], q_pe[0:64, 2 * g:2 * g + 2, 0:TL],
                                  start=True, stop=True).then_inc(sem("rope_ps"), 1)

            def attention(name, units, scores, pv, pr, filler):
                s_ = lambda k: sem(f"{name}_{k}")
                tb, ob = (2, 4) if name == "mla" else (4, 6)
                pt = pt_e if name == "mla" else pt_o
                for i in range(len(units) + 3):
                    if i < len(units):
                        if i >= 2:
                            pe.wait_ge(s_("exp"), i - 1)
                        scores(i).then_inc(s_("scores"), 1)
                    filler(i)
                    if 2 <= i <= len(units) + 1:
                        u = i - 2
                        pe.wait_ge(s_("probs"), u + 1)
                        if u >= 2:
                            pe.wait_ge(s_("pt"), u - 1)
                        for b in range(units[u][2] // P):
                            mm = pe.transpose(ps[:, tb + u % 2, b * P:(b + 1) * P], pr(u, b), ident)
                        mm.then_inc(s_("turned"), 1)
                    if i >= 3:
                        u = i - 3
                        pe.wait_ge(s_("pt"), u + 1)
                        if u >= 2:
                            pe.wait_ge(s_("out"), u - 1)
                        nb = units[u][2] // P
                        for b in range(nb):
                            mm = pe.matmul(ps[:, ob + u % 2, 0:P], pv(u, b), pt[:, u % 2, b * P:(b + 1) * P],
                                           start=(b == 0), stop=(b == nb - 1))
                        mm.then_inc(s_("pv"), 1)

            units = mla_units()
            pe.wait_ge(sem("proj_ready"), len(jobs))
            pe.wait_ge(sem("rope_done"), 3)

            def scores_e(i):
                h, j, n, k0 = units[i]
                pe.matmul(ps[:, i % 2, 0:n], q_nope[:, h, j * P:(j + 1) * P], k_nope[:, h, k0:k0 + n], start=True, stop=False)
                return pe.matmul(ps[:, i % 2, 0:n], q_pe[0:64, h, j * P:(j + 1) * P], k_pe[0:64, k0:k0 + n],
                                 start=False, stop=True)

            attention("mla", units, scores_e,
                      lambda u, b: v_e[:, units[u][3] // P + b, units[u][0] * P:(units[u][0] + 1) * P],
                      lambda u, b: pr_e[:, u % 2, b * P:(b + 1) * P], lambda i: filler(MOD_GAP + 4 + i))
            mod_cols(N_MOD - 1)
            pe.wait_ge(sem("mla_out"), len(units))
            pe.wait_ge(sem("mla_pt"), len(units))
            out_pieces(S_WOUT, T, N_EY)
            sum_squares(N_E2)
            for m in range(NF):
                piece(S_GU + m, T, (lambda k: pe.wait_ge(mod_lo, KD + k + 1)) if m == 0 else None)

            pe.wait_ge(evac_dve, evacs(S_GU + NF - 1, "dve"))
            for f in range(NF):
                s = S_DOWN + f // 2
                if f % 2 == 0:
                    pe.wait_ge(w_lo, s + 1)
                pe.wait_ge(sem("hid_lo"), f + 1)
                for m in range(KD):
                    at = (f % 2) * D + m * P
                    mm = mm3(ps[:, m, :], wh[:, s % SPLITS, at:at + P], wl[:, s % SPLITS, at:at + P],
                             sh[:, f % 2, :], sl[:, f % 2, :], f == 0, f == NF - 1)
                mm.then_inc(w_used if f % 2 else sem("f_used"), 1)
            pe.wait_ge(sem("y2_dve"), 1)
            sum_squares(N_EF)
            sum_squares(N_O1)

            def turn(p):
                src = q_o[:, 2 * p:2 * p + 2, :] if p < 3 else k_o[:, 2 * p - 6:2 * p - 4, 0:TL]
                pe.wait_ge(evac_act, evacs(S_OIN + p, "act"))
                if p >= 2:
                    pe.wait_ge(sem("orope_done"), p - 1)
                else:
                    pe.wait_ge(root_ready, N_O1 + 1)
                pe.matmul(ps[:, 4 + (p + 1) % 2, :], rot, src, start=True, stop=True).then_inc(sem("orope_ps"), 1)

            for p in range(10):
                W = T if 3 <= p < 6 else TL
                piece(S_OIN + p, W, (lambda k: pe.wait_ge(mod_lo, 2 * KD + k + 1)) if p == 0 else None, tokens=(6 <= p < 9))
                if 1 <= p <= 6:
                    turn(p - 1)
            pe.wait_ge(sem("dftc_loaded"), 16)
            pe.wait_ge(sem("dftt_loaded"), 16)
            pe.wait_ge(evac_act, evacs(S_OIN + 9, "act"))
            for t in range(2):
                for c in range(2):
                    mm = pe.matmul(ps[:, t, c * 256:(c + 1) * 256], f_o[:, c, t * P:(t + 1) * P], dftc, start=True, stop=True)
            mm.then_inc(sem("four_ps"), 1)
            pe.wait_ge(sem("four_mid"), 1)
            for c in range(2):
                for n in range(4):
                    t, part = n // 2, n % 2
                    mm = pe.matmul(ps[:, 2, c * TL:(c + 1) * TL], mid[:, 2 * t + c, part * P:(part + 1) * P],
                                   dftt[:, 2 * t + part, :], start=(n == 0), stop=(n == 3))
            mm.then_inc(sem("four_ps"), 1)

            ounits = diff_units()
            pe.wait_ge(sem("four_lo"), 1)
            pe.wait_ge(sem("orope_done"), 6)

            def scores_o(i):
                h, j, n, _ = ounits[i]
                for m in range(2):
                    mm = pe.matmul(ps[:, 2 * (i % 2) + m, :], q_o[64 * m:64 * m + 64, h, j * P:(j + 1) * P],
                                   k_o[64 * m:64 * m + 64, h, :], start=True, stop=True)
                return mm

            def head_sums(n):
                pe.wait_ge(sem("osq_ready"), n + 1)
                pe.matmul(ps[:, HEAD_SUMS[n], :], ones, o_sq[:, 2 * n:2 * n + 2, :], start=True, stop=True).then_inc(sem("ossq_done"), 1)

            def early_norms(i):
                if i == len(ounits) + 1:
                    pe.wait_ge(sem("diff_exp"), len(ounits))
                    for n in range(DH // 2 - 1):
                        head_sums(n)

            attention("diff", ounits, scores_o, lambda u, b: v_o[:, b, ounits[u][0] * P:(ounits[u][0] + 1) * P],
                      lambda u, b: pr_o[:, u % 2, 0, b * P:(b + 1) * P], early_norms)
            head_sums(DH // 2 - 1)
            out_pieces(S_OOUT, TL, N_OY, lambda k: pe.wait_ge(sem("o_lo"), min(k + 1, DH)))
            sum_squares(N_O2)

            pe.wait_ge(mod_h, 3 * 2 * KD + KD)
            pe.wait_ge(root_ready, N_O2 + 1)
            router = vc("router").rearrange("p (k e) -> p k e", k=KD)
            for t in range(2):
                for k in range(KD):
                    mm = pe.matmul(ps[:, 4, 8 * t:8 * t + 8], h2f[:, k, t * P:(t + 1) * P], router[:, k, :],
                                   start=(k == 0), stop=(k == KD - 1))
            mm.then_inc(sem("logits_ps"), 1)
            for t in range(2):
                for k in range(KD):
                    mm = pe.transpose(ps[:, 2 * t + k // 4, (k % 4) * P:(k % 4 + 1) * P], h2f[:, k, t * P:(t + 1) * P], ident)
                mm.then_inc(sem("tok_ps"), 1)
            pe.wait_ge(sem("mask_ready"), 1)
            mask = [small[:, 32 + 8 * t:40 + 8 * t] for t in range(2)]
            pe.matmul(ps[:, 4, 16:24], tri, mask[0], start=True, stop=True)
            pe.matmul(ps[:, 4, 24:32], ones, mask[0], start=True, stop=False)
            pe.matmul(ps[:, 4, 24:32], tri, mask[1], start=False, stop=True)
            pe.matmul(ps[:, 4, 32:40], ones, mask[0], start=True, stop=False)
            pe.matmul(ps[:, 4, 32:40], ones, mask[1], start=False, stop=True).then_inc(sem("rank_ps"), 1)
            pe.wait_ge(sem("tok_lo"), 2)
            pe.wait_ge(sem("count_ready"), 1)

            def gather(idx):
                pe.wait_ge(sem("sel_ready"), idx)
                for src, bank, done in ((h2h, 6, "xh_ps"), (h2l, 1, "xl_ps")):
                    for k in range(KD):
                        for t in range(2):
                            mm = pe.matmul(ps[:, bank + k // 4, (k % 4) * P:(k % 4 + 1) * P],
                                           src[:, t, k * P:(k + 1) * P], sel[:, t, :], start=(t == 0), stop=(t == 1))
                    mm.then_inc(sem(done), 1)

            def experts(no):
                at = Pass(no)

                def gate_up(J, g, half, e):
                    b = J % SPLITS
                    pe.wait_ge(w_lo, PER_EXPERT * e + (S_MOE + J + 1))
                    for k in range(4):
                        kk = 4 * half + k
                        mm = mm3(ps[:, g % 2, :], xeh[:, kk, :], xel[:, kk, :], wh[:, b, k * 512:(k + 1) * 512],
                                 wl[:, b, k * 512:(k + 1) * 512], kk == 0, kk == KD - 1)
                    mm.then_inc(w_used, 1)

                def down(J, g, e):
                    b = J % SPLITS
                    pe.wait_ge(w_lo, PER_EXPERT * e + (S_MOE + J + 1))
                    pe.wait_ge(sem("hT_lo"), 11 * e + (at.turned + g + 1))
                    for f in range(2):
                        for c in range(2):
                            w0 = f * D + c * 512
                            mm = mm3(ps[:, 3 + c, :], sh[:, g % 2, f * P:(f + 1) * P], sl[:, g % 2, f * P:(f + 1) * P],
                                     wh[:, b, w0:w0 + 512], wl[:, b, w0:w0 + 512], g == 0 and f == 0, g == 10 and f == 1)
                    mm.then_inc(w_used, 1)

                def turn_hidden(g, count):
                    pe.wait_ge(sem("moe_hid"), count)
                    for b in range(2):
                        mm = pe.transpose(ps[:, 5, b * P:(b + 1) * P], hh(g)[:, b * P:(b + 1) * P], ident)
                    mm.then_inc(sem("hid_T"), 1)

                def scatter(e):
                    pe.wait_ge(sem("y_l"), e + (at.results + 1))
                    for c in range(4):
                        for k in (2 * c, 2 * c + 1):
                            out = ps[:, SCATTER[c], (k % 2) * TL:(k % 2 + 1) * TL]
                            pe.matmul(out, yh[:, k * P:(k + 1) * P], selT, start=True, stop=False)
                            mm = pe.matmul(out, yl[:, k * P:(k + 1) * P], selT, start=False, stop=True)
                        mm.then_inc(sem("scat_ps"), 1)

                pe.wait_ge(sem("acc_done"), at.added)
                gather(at.gathered + 1)
                pe.wait_ge(sem("xe_h"), at.gathered + 1)
                pe.wait_ge(sem("xe_l"), at.gathered + 1)
                for half in range(2):
                    gate_up(at.J + half, 0, half, 0)
                turn_hidden(0, at.hid + 1)
                with pe.Fori(0, NE) as e:
                    for q, (kind, g, half) in enumerate(ORDER):
                        J = at.J + 2 + q
                        if q == 30:
                            pe.wait_ge(sem("xe_h"), e + (at.gathered + 2))
                            pe.wait_ge(sem("xe_l"), e + (at.gathered + 2))
                        if kind == "gu":
                            gate_up(J, g, half, e)
                        else:
                            down(J, g, e)
                        if q == 1:
                            scatter(e)
                        if q == 2:
                            pe.wait_ge(sem("acc_done"), 4 * e + (at.added + 1))
                        if q == 5:
                            pe.wait_ge(sem("acc_done"), 4 * e + (at.added + 4))
                            for t in range(2):
                                pe.transpose(ps[:, 2, t * P:(t + 1) * P], sel[:, t, :].bitcast(F32), ident)
                            pe.matmul(ps[:, 2, TL:TL + 1], sel[:, 0, :].bitcast(F32), cur[:, 2:3], start=True, stop=False)
                            pe.matmul(ps[:, 2, TL:TL + 1], sel[:, 1, :].bitcast(F32), cur[:, 3:4], start=False, stop=True
                                      ).then_inc(sem("selT_ps"), 1)
                        if q == GATHER:
                            pe.wait_ge(sem("selT_ready"), e + (at.selT + 1))
                            pe.wait_ge(sem("moe_hid"), 11 * e + (at.hid + 10))
                            gather(e + (at.gathered + 2))
                            pe.wait_ge(sem("hT_lo"), 11 * e + (at.turned + 9))
                        if q in TURN:
                            turn_hidden(TURN[q], 11 * e + (at.hid + (TURN[q] or 11) + 1))
                scatter(NE)

            experts(0)
            most = pe.value_load(cnt[0:1, 0:1], min_val=0, max_val=TL)
            with pe.If(most > P):
                experts(1)
            sum_squares(N_OF)


def mla_units():
    return [(h, j, T if j < 2 else TL, 0 if j < 2 else TL) for h in range(HEADS) for j in range(4)]


def diff_units():
    return [(h, j, T, 0) for h in range(DH) for j in range(2)]


def _chunked(w):
    return w.reshape(-1, P, w.shape[-1]).transpose(1, 0, 2)


def _columns(w):
    n = w.shape[1] // 256
    return w.reshape(KD, P, n, 256).transpose(2, 1, 0, 3).reshape(n, P, PIECE)


def _rows(w):
    n = w.shape[0] // 256
    return w.reshape(n, 2, P, D).transpose(0, 2, 1, 3).reshape(n, P, PIECE)


def _constants():
    cst = np.zeros((P, 5, P), np.float32)
    r = np.arange(P)
    cst[r, 0, r] = 1.0
    cst[:, 1, :] = 1.0
    cst[:, 2, :] = r[:, None] < r[None, :]
    cst[:, 3, :] = r[None, :]
    for m in range(P):
        if m % 64 < 32:
            cst[m + 32, 4, m] = -1.0
        else:
            cst[m - 32, 4, m] = 1.0
    t = np.arange(TL)
    inv = (np.float32(10000.0) ** (-np.arange(16, dtype=np.float32) / np.float32(16))).astype(np.float32)
    row, col = (t // 64).astype(np.float32), (t % 64).astype(np.float32)
    ang = np.concatenate([row[:, None] * inv, col[:, None] * inv], -1)
    ang = ang.T[r % 32]
    rope = np.stack([np.cos(ang), np.sin(ang)], 1).astype(np.float32)
    c = np.arange(64)
    a = 2 * np.pi * ((c[:, None] * c[None, :]) % 64) / 64
    dft = np.zeros((P, 1280), np.float32)
    for g in range(2):
        dft[g * 64:(g + 1) * 64, g * 64:(g + 1) * 64] = np.cos(a)
        dft[g * 64:(g + 1) * 64, P + g * 64:P + (g + 1) * 64] = np.sin(a)
    a = 2 * np.pi * ((t[:, None] * t[None, :]) % TL) / TL
    norm = math.sqrt(TL * 64)
    both = np.stack([np.cos(a), -np.sin(a)]) / norm
    dft[:, 256:] = both.reshape(2, 2, P, TL).transpose(2, 1, 0, 3).reshape(P, 1024)
    return cst, rope, dft


def kernel(x, c, ctx, c_ctx, ev_mod_w, ev_mod_b, ev_norm_g, ev_w_in, ev_conv_w, ev_q_norm_g, ev_w_uq,
           ev_kv_norm_g, ev_w_ukv, ev_w_out, ev_ffn_gate, ev_ffn_up, ev_ffn_down, od_mod_w, od_mod_b,
           od_norm_g, od_w_in, od_lambda, od_subln_g, od_w_out, od_router, od_exp_gate, od_exp_up, od_exp_down):
    import concourse.bacc as _bacc
    from concourse.bass_utils import run_bass_kernel_spmd as _run

    A = np.asarray
    xT = _chunked(np.concatenate([A(x)[0], A(ctx)[0]], 0).T)
    per_part = lambda v: A(v).reshape(-1, P).T
    twice = lambda v: np.repeat(per_part(v)[:, :, None], 2, 2).reshape(P, -1)
    lam = np.zeros((P, 4), np.float32)
    lam[0:64] = A(od_lambda)[0].T
    vec = np.concatenate([
        np.stack([per_part(A(c)[0]), per_part(A(c_ctx))], 2).reshape(P, 16),
        twice(A(ev_mod_b)[0]), twice(A(od_mod_b)[0]), twice(A(ev_norm_g)[0]), twice(A(od_norm_g)[0]),
        A(ev_conv_w)[0].reshape(3, 4, P).transpose(2, 0, 1).reshape(P, 12),
        per_part(A(ev_q_norm_g)[0]), per_part(A(ev_kv_norm_g)[0]), per_part(A(od_subln_g)[0]), lam,
        _chunked(A(od_router)[0]).reshape(P, 64)], 1)
    cst, rope, dft = _constants()

    stream = np.empty((S_MOE + MOE_STREAM, P, PIECE), np.float32)
    mod = np.concatenate([_columns(A(ev_mod_w)[0]), _columns(A(od_mod_w)[0])])
    for n in range(N_MOD):
        stream[s_mod(n)] = mod[n]
    w = A(ev_w_in)[0]
    order = [w[:, 0:512]]
    for j in range(4):
        order += [w[:, 512 + j * P:640 + j * P], w[:, 1024 + j * P:1152 + j * P]]
    order += [w[:, 1536:], np.zeros((D, 64), np.float32)]
    stream[MOD_FIRST:s_win(WIN):3] = _columns(np.concatenate(order, 1))
    at = S_WOUT
    g, u = (A(v)[0].reshape(D, NF, 1, P) for v in (ev_ffn_gate, ev_ffn_up))
    for part in (_columns(A(ev_w_out)[0]), _columns(np.concatenate([g, u], 2).reshape(D, 2 * FF)), _rows(A(ev_ffn_down)[0]),
                 _columns(A(od_w_in)[0]), _columns(A(od_w_out)[0])):
        stream[at:at + len(part)] = part
        at += len(part)
    gate, up, down = A(od_exp_gate)[0], A(od_exp_up)[0], A(od_exp_down)[0]
    pieces = stream[S_MOE:]
    for e in range(NE):
        both = np.stack([gate[e].reshape(D, NF, P), up[e].reshape(D, NF, P)], 2)
        both = both.reshape(2, 4, P, 11, 512).transpose(3, 0, 2, 1, 4).reshape(11, 2, P, PIECE)
        rows = _rows(down[e])
        own = pieces[2 + e * PER_EXPERT:2 + (e + 1) * PER_EXPERT]
        for q, (kind, g, half) in enumerate(ORDER):
            if kind == "d":
                own[q] = rows[g]
            elif g:
                own[q] = both[g, half]
        first = pieces[0:2] if e == 0 else pieces[PER_EXPERT * e - 1:PER_EXPERT * e + 1]
        first[:] = both[0]
    pieces[PER_EXPERT * NE - 1:PER_EXPERT * NE + 1] = pieces[0:2]
    pieces[2 + PER_EXPERT * NE:] = pieces[0:AHEAD]

    arrays = {"x": xT, "vec": vec, "cst": cst, "rope": rope, "dft": dft, "uq": _chunked(A(ev_w_uq)[0]),
              "ukv": _chunked(A(ev_w_ukv)[0]), "w": stream}
    arrays = {f"in_{n}": np.ascontiguousarray(v) for n, v in arrays.items()}
    nc = _bacc.Bacc("TRN2", target_bir_lowering=False, num_devices=1)
    aps = [nc.dram_tensor(n, v.shape, mybir.dt.from_np(v.dtype), kind="ExternalInput").ap() for n, v in arrays.items()]
    out = nc.dram_tensor("out", (P, KD, TL), F32, kind="ExternalOutput").ap()
    build(nc, *aps, out)
    r = _run(nc, [arrays], core_ids=[0])
    return r.results[0]["out"].transpose(2, 1, 0).reshape(1, TL, D)
```
